# Optimizing a Trainium2 kernel written in Bass

```python
import jax, jax.numpy as jnp
from jax import lax
import numpy as np

D_MODEL = 1024
BATCH = 1
SEQ = 256
DEPTH = 2

N_MIXERS = 2
N_SSD_LAYERS = (DEPTH + 1) // 2
N_HGRN_LAYERS = DEPTH // 2
NORM_EPS = 1e-6

SSD_EXPAND = 2
SSD_D_INNER = SSD_EXPAND * D_MODEL
SSD_HEAD_DIM = 64
SSD_N_HEADS = SSD_D_INNER // SSD_HEAD_DIM
SSD_N_GROUPS = 4
SSD_HEADS_PER_GROUP = SSD_N_HEADS // SSD_N_GROUPS
SSD_D_STATE = 128
SSD_CONV_WIDTH = 4
SSD_CONV_DIM = SSD_D_INNER + 2 * SSD_N_GROUPS * SSD_D_STATE
SSD_IN_DIM = SSD_D_INNER + SSD_CONV_DIM + SSD_N_HEADS
SSD_NORM_GROUP = SSD_D_INNER // SSD_N_GROUPS
SSD_CHUNK = 128

HGRN_EXPAND = 128
HGRN_N_HEADS = D_MODEL // HGRN_EXPAND
HGRN_K_DIM = HGRN_EXPAND
HGRN_V_DIM = D_MODEL // HGRN_N_HEADS
HGRN_FORGET_DIM = HGRN_N_HEADS * HGRN_K_DIM
HGRN_IN_DIM = 2 * HGRN_FORGET_DIM + 2 * D_MODEL
HGRN_CHUNK = 64

PEER_N_KEYS = 128
PEER_N_EXPERTS = PEER_N_KEYS * PEER_N_KEYS
PEER_N_HEADS = 8
PEER_D_QUERY = 256
PEER_D_HALF = PEER_D_QUERY // 2
PEER_TOPK = 16
PEER_TOKEN_BLOCK = 128

kernel_name = 'hybrid_ssd_hgrn2_peer'

def rmsnorm(x, g):
    xf = x.astype(jnp.float32)
    r = lax.rsqrt(jnp.mean(xf * xf, axis=-1, keepdims=True) + NORM_EPS)
    return (xf * r).astype(x.dtype) * g

def to_chunks(t, length):
    b, s = t.shape[0], t.shape[1]
    return jnp.moveaxis(t.reshape((b, s // length, length) + t.shape[2:]), 1, 0)

def from_chunks(t):
    t = jnp.moveaxis(t, 0, 1)
    return t.reshape((t.shape[0], t.shape[1] * t.shape[2]) + t.shape[3:])

def causal_depthwise_conv(x, w, b):
    c = x.shape[-1]
    y = lax.conv_general_dilated(x, w[:, None, :].astype(x.dtype), window_strides=(1,),
                                 padding=[(SSD_CONV_WIDTH - 1, 0)],
                                 dimension_numbers=('NWC', 'WIO', 'NWC'),
                                 feature_group_count=c)
    return y + b

def ssd_chunked_scan(x, dt, a, bm, cm):
    bsz, _, g, hg, p = x.shape
    n = bm.shape[-1]
    mask = jnp.tril(jnp.ones((SSD_CHUNK, SSD_CHUNK), bool))[None, :, :, None, None]

    def step(state, inp):
        xc, dtc, bc, cc = inp
        acs = jnp.cumsum(dtc * a, axis=1)
        seg = acs[:, :, None] - acs[:, None, :]
        decay = jnp.exp(jnp.where(mask, seg, -jnp.inf))
        cb = jnp.einsum('blgn,bsgn->blsg', cc, bc)
        w = cb[..., None] * decay * dtc[:, None]
        y = jnp.einsum('blsgh,bsghp->blghp', w, xc)
        y = y + jnp.einsum('blgn,bghpn->blghp', cc, state) * jnp.exp(acs)[..., None]
        tail = jnp.exp(acs[:, -1:] - acs) * dtc
        state = (state * jnp.exp(acs[:, -1])[..., None, None]
                 + jnp.einsum('bsgh,bsgn,bsghp->bghpn', tail, bc, xc))
        return state, y

    state0 = jnp.zeros((bsz, g, hg, p, n), jnp.float32)
    _, ys = lax.scan(step, state0, (to_chunks(x, SSD_CHUNK), to_chunks(dt, SSD_CHUNK),
                                    to_chunks(bm, SSD_CHUNK), to_chunks(cm, SSD_CHUNK)))
    return from_chunks(ys)

def ssd_mixer(h, w_in, conv_w, conv_b, dt_bias, a_log, d_skip, norm_g, w_out):
    bsz, s, _ = h.shape
    g, hg, p, n = SSD_N_GROUPS, SSD_HEADS_PER_GROUP, SSD_HEAD_DIM, SSD_D_STATE
    z, xbc, dt = jnp.split(h @ w_in, [SSD_D_INNER, SSD_D_INNER + SSD_CONV_DIM], axis=-1)
    xbc = jax.nn.silu(causal_depthwise_conv(xbc, conv_w, conv_b))
    xs, bm, cm = jnp.split(xbc, [SSD_D_INNER, SSD_D_INNER + g * n], axis=-1)
    xs = xs.reshape(bsz, s, g, hg, p).astype(jnp.float32)
    bm = bm.reshape(bsz, s, g, n).astype(jnp.float32)
    cm = cm.reshape(bsz, s, g, n).astype(jnp.float32)
    dt = jax.nn.softplus((dt + dt_bias).astype(jnp.float32)).reshape(bsz, s, g, hg)
    a = -jnp.exp(a_log.astype(jnp.float32)).reshape(g, hg)
    y = ssd_chunked_scan(xs, dt, a, bm, cm)
    y = y + xs * d_skip.astype(jnp.float32).reshape(g, hg, 1)
    y = y.astype(h.dtype).reshape(bsz, s, SSD_D_INNER) * jax.nn.silu(z)
    y = rmsnorm(y.reshape(bsz, s, g, SSD_NORM_GROUP), norm_g.reshape(g, SSD_NORM_GROUP))
    return y.reshape(bsz, s, SSD_D_INNER) @ w_out

def hgrn2_chunked(q, k, v, log_f):
    bsz, _, hh, kd = q.shape
    vd = v.shape[-1]
    mask = jnp.tril(jnp.ones((HGRN_CHUNK, HGRN_CHUNK), bool))[None, :, :, None, None]

    def step(state, inp):
        qc, kc, vc, gc = inp
        bcum = jnp.cumsum(gc, axis=1)
        seg = bcum[:, :, None] - bcum[:, None, :]
        decay = jnp.exp(jnp.where(mask, seg, -jnp.inf))
        att = jnp.einsum('blhk,bshk,blshk->blsh', qc, kc, decay)
        o = jnp.einsum('blsh,bshv->blhv', att, vc)
        o = o + jnp.einsum('blhk,bhkv->blhv', qc * jnp.exp(bcum), state)
        tail = kc * jnp.exp(bcum[:, -1:] - bcum)
        state = (state * jnp.exp(bcum[:, -1])[..., None]
                 + jnp.einsum('bshk,bshv->bhkv', tail, vc))
        return state, o

    state0 = jnp.zeros((bsz, hh, kd, vd), jnp.float32)
    _, os_ = lax.scan(step, state0, (to_chunks(q, HGRN_CHUNK), to_chunks(k, HGRN_CHUNK),
                                     to_chunks(v, HGRN_CHUNK), to_chunks(log_f, HGRN_CHUNK)))
    return from_chunks(os_)

def hgrn_lower_bound(lb_logits, layer):
    p = jax.nn.softmax(lb_logits.astype(jnp.float32), axis=0)
    return jnp.cumsum(p, axis=0)[layer] - p[0]

def hgrn2_mixer(h, w_in, lower_bound, norm_g, w_out):
    bsz, s, _ = h.shape
    hh, kd, vd = HGRN_N_HEADS, HGRN_K_DIM, HGRN_V_DIM
    q, f, i, g = jnp.split(h @ w_in, [HGRN_FORGET_DIM, 2 * HGRN_FORGET_DIM,
                                      2 * HGRN_FORGET_DIM + D_MODEL], axis=-1)
    q = q.reshape(bsz, s, hh, kd).astype(jnp.float32)
    fl = f.reshape(bsz, s, hh, kd).astype(jnp.float32)
    i = i.reshape(bsz, s, hh, vd).astype(jnp.float32)
    lb = lower_bound.reshape(hh, kd)
    forget = lb + (1.0 - lb) * jax.nn.sigmoid(fl)
    log_f = jnp.log(forget)
    k = (1.0 - lb) * jax.nn.sigmoid(-fl)
    o = hgrn2_chunked(q, k, i, log_f).astype(h.dtype)
    o = rmsnorm(o, norm_g) * jax.nn.silu(g.reshape(bsz, s, hh, vd))
    return o.reshape(bsz, s, D_MODEL) @ w_out

def peer_ffn(h, w_query, sub_keys, expert_u, expert_v):
    bsz, s, d = h.shape
    nb = PEER_TOKEN_BLOCK
    blocks = h.reshape((bsz * s) // nb, nb, d)

    def one_block(xb):
        q = (xb @ w_query).reshape(nb, PEER_N_HEADS, 2, PEER_D_HALF)
        sc = jnp.einsum('nhcd,hckd->nhck', q, sub_keys).astype(jnp.float32)
        top_s, top_i = lax.top_k(sc, PEER_TOPK)
        cand_s = (top_s[:, :, 0, :, None] + top_s[:, :, 1, None, :]).reshape(nb, PEER_N_HEADS, -1)
        cand_i = (top_i[:, :, 0, :, None] * PEER_N_KEYS + top_i[:, :, 1, None, :]).reshape(nb, PEER_N_HEADS, -1)
        best_s, best_pos = lax.top_k(cand_s, PEER_TOPK)
        idx = jnp.take_along_axis(cand_i, best_pos, axis=-1)
        gate = jax.nn.softmax(best_s, axis=-1).astype(xb.dtype)
        u = expert_u[idx]
        v = expert_v[idx]
        act = jax.nn.gelu(jnp.einsum('nhkd,nd->nhk', u, xb), approximate=False)
        return jnp.einsum('nhk,nhkd->nd', gate * act, v)

    return lax.map(one_block, blocks).reshape(bsz, s, d)

def setup_inputs(seed: int = 0) -> dict:
    key = jax.random.key(seed)
    ks = jax.random.split(key, 24)
    f32 = jnp.float32
    nrm = lambda k, shape, scale: jax.random.normal(k, shape, f32) * scale
    x = jax.random.normal(ks[0], (BATCH, SEQ, D_MODEL), f32)
    mix_norm_g = 1.0 + nrm(ks[1], (DEPTH, D_MODEL), 0.02)
    ffn_norm_g = 1.0 + nrm(ks[2], (DEPTH, D_MODEL), 0.02)
    final_norm_g = 1.0 + nrm(ks[3], (D_MODEL,), 0.02)
    ssd_w_in = nrm(ks[4], (N_SSD_LAYERS, D_MODEL, SSD_IN_DIM), D_MODEL ** -0.5)
    ssd_conv_w = nrm(ks[5], (N_SSD_LAYERS, SSD_CONV_WIDTH, SSD_CONV_DIM), SSD_CONV_WIDTH ** -0.5)
    ssd_conv_b = nrm(ks[6], (N_SSD_LAYERS, SSD_CONV_DIM), 0.02)
    dt0 = jnp.exp(jax.random.uniform(ks[7], (N_SSD_LAYERS, SSD_N_HEADS), f32,
                                     jnp.log(1e-3), jnp.log(1e-1)))
    ssd_dt_bias = dt0 + jnp.log(-jnp.expm1(-dt0))
    ssd_a_log = jnp.log(jax.random.uniform(ks[8], (N_SSD_LAYERS, SSD_N_HEADS), f32, 1.0, 16.0))
    ssd_d_skip = 1.0 + nrm(ks[9], (N_SSD_LAYERS, SSD_N_HEADS), 0.02)
    ssd_norm_g = 1.0 + nrm(ks[10], (N_SSD_LAYERS, SSD_D_INNER), 0.02)
    ssd_w_out = nrm(ks[11], (N_SSD_LAYERS, SSD_D_INNER, D_MODEL), SSD_D_INNER ** -0.5)
    hgrn_w_in = nrm(ks[12], (N_HGRN_LAYERS, D_MODEL, HGRN_IN_DIM), D_MODEL ** -0.5)
    hgrn_lb_logits = 1.0 + nrm(ks[13], (DEPTH, HGRN_FORGET_DIM), 0.1)
    hgrn_norm_g = 1.0 + nrm(ks[14], (N_HGRN_LAYERS, HGRN_V_DIM), 0.02)
    hgrn_w_out = nrm(ks[15], (N_HGRN_LAYERS, D_MODEL, D_MODEL), D_MODEL ** -0.5)
    peer_w_query = nrm(ks[16], (DEPTH, D_MODEL, PEER_N_HEADS * PEER_D_QUERY), D_MODEL ** -0.5)
    peer_sub_keys = nrm(ks[17], (DEPTH, PEER_N_HEADS, 2, PEER_N_KEYS, PEER_D_HALF), PEER_D_HALF ** -0.5)
    peer_u = nrm(ks[18], (DEPTH, PEER_N_EXPERTS, D_MODEL), D_MODEL ** -0.5)
    peer_v = nrm(ks[19], (DEPTH, PEER_N_EXPERTS, D_MODEL), PEER_N_HEADS ** -0.5)
    return {'x': x, 'mix_norm_g': mix_norm_g, 'ffn_norm_g': ffn_norm_g,
            'final_norm_g': final_norm_g, 'ssd_w_in': ssd_w_in, 'ssd_conv_w': ssd_conv_w,
            'ssd_conv_b': ssd_conv_b, 'ssd_dt_bias': ssd_dt_bias, 'ssd_a_log': ssd_a_log,
            'ssd_d_skip': ssd_d_skip, 'ssd_norm_g': ssd_norm_g, 'ssd_w_out': ssd_w_out,
            'hgrn_w_in': hgrn_w_in, 'hgrn_lb_logits': hgrn_lb_logits,
            'hgrn_norm_g': hgrn_norm_g, 'hgrn_w_out': hgrn_w_out,
            'peer_w_query': peer_w_query, 'peer_sub_keys': peer_sub_keys,
            'peer_u': peer_u, 'peer_v': peer_v}

def reference(x, mix_norm_g, ffn_norm_g, final_norm_g, ssd_w_in, ssd_conv_w, ssd_conv_b,
              ssd_dt_bias, ssd_a_log, ssd_d_skip, ssd_norm_g, ssd_w_out, hgrn_w_in,
              hgrn_lb_logits, hgrn_norm_g, hgrn_w_out, peer_w_query, peer_sub_keys,
              peer_u, peer_v):
    for layer in range(DEPTH):
        h = rmsnorm(x, mix_norm_g[layer])
        j = layer // N_MIXERS
        if layer % N_MIXERS == 0:
            x = x + ssd_mixer(h, ssd_w_in[j], ssd_conv_w[j], ssd_conv_b[j], ssd_dt_bias[j],
                              ssd_a_log[j], ssd_d_skip[j], ssd_norm_g[j], ssd_w_out[j])
        else:
            lb = hgrn_lower_bound(hgrn_lb_logits, layer)
            x = x + hgrn2_mixer(h, hgrn_w_in[j], lb, hgrn_norm_g[j], hgrn_w_out[j])
        h = rmsnorm(x, ffn_norm_g[layer])
        x = x + peer_ffn(h, peer_w_query[layer], peer_sub_keys[layer], peer_u[layer], peer_v[layer])
    return rmsnorm(x, final_norm_g)


_drawn_inputs = setup_inputs


def setup_inputs(seed=0):
    import zlib

    import numpy as np

    out = dict(_drawn_inputs(seed))
    spreads = {}
    factors = {}
    for name, (base, spread) in spreads.items():
        noise = np.random.default_rng([zlib.crc32(name.encode()), seed]).standard_normal(out[name].shape)
        drawn = base * np.exp(spread * noise) if base else spread * noise
        out[name] = __import__('jax').numpy.asarray(drawn.astype(out[name].dtype))
    for name, factor in factors.items():
        out[name] = (out[name] * factor).astype(out[name].dtype)
    return out
```

```python
from contextlib import ExitStack

import concourse.bass as bass
from concourse import mybir

F32 = mybir.dt.float32
F32R = mybir.dt.float32r
U32 = mybir.dt.uint32
ALU = mybir.AluOpType
ACT = mybir.ActivationFunctionType
AX = mybir.AxisListType

P = 128
D = 1024
KC = D // P
T = 256
NB = T // P
TILE = KC * P
EPS = 1e-6

SSD_TILES = 40
CONV = 24
XT = 16
HEADS = 32
GROUPS = 4
HGRN_HEADS = 8
HCHUNK = 64
PH = 8
KEYS = 128
TOPK = 16

RAW = 4
SPL = 4
BANKS = 4

STREAM = [("ssd_in", SSD_TILES), ("ssd_out", 16), ("q0", 16), ("u0", 128), ("v0", 128),
          ("hgrn_in", 32), ("hgrn_out", 8), ("q1", 16), ("u1", 128), ("v1", 128)]
FIRST, POOL_LO, DVE_LO = {}, {}, {}
EVAC = {}
_g = _p = _d = _e = 0
for _n, _c in STREAM:
    FIRST[_n], POOL_LO[_n], DVE_LO[_n], EVAC[_n] = _g, _p, _d, _e
    _g += _c
    if _n[0] == "v":
        _d += _c
    else:
        _p += _c
        _e += 0 if _n == "ssd_out" else _c
COUNT = dict(STREAM)
STAGES = [n for n, _ in STREAM]

PAR = {}
_at = 0
for _n, _c in [("norm_g", 5 * KC), ("conv_w", CONV * 4), ("conv_b", CONV), ("d_skip", XT), ("ssd_g", XT),
               ("lb", 2 * KC), ("hgrn_g", 1), ("dt_bias", 1), ("a_log", 1)]:
    PAR[_n] = (_at, _at + _c)
    _at += _c
NPAR = _at

LEVELS = [1, 2, 4, 8, 16, 32, 64]
CON = {"ident": 0, "iota": 1, "tri": 2, "lev": 3}
NCON = 3 + len(LEVELS)

ACTS = {"ssd_in": 1, "y0": 2, "y1": 3, "q0": 4, "hgrn_in": 5, "hgrn_out": 6, "q1": 7}
SCRATCH0 = 72


def trunk(nc, x_t, par, con, w_dt, weights, sub_keys, out_t):
    ctx = ExitStack()

    def sb(name, shape, dt=F32):
        return ctx.enter_context(nc.sbuf_tensor(name, shape, dt))

    def sem(name):
        return ctx.enter_context(nc.semaphore(name))

    with ctx:
        big = sb("big", [P, 128, T])
        raw = sb("raw", [P, RAW, KC, P])
        whi = sb("whi", [P, SPL, KC, P], F32R)
        wlo = sb("wlo", [P, SPL, KC, P], F32R)
        x = sb("x", [P, KC, T])
        hhi = sb("hhi", [P, KC, T], F32R)
        hlo = sb("hlo", [P, KC, T], F32R)
        pars = sb("pars", [P, NPAR])
        ident = sb("ident", [P, P])
        iota = sb("iota", [P, P])
        ones = sb("ones", [P, P])
        zero = sb("zero", [P, 512], mybir.dt.bfloat16)
        picks = sb("picks", [P, 3, T])
        oha = sb("oha", [P, 2, 4, P])
        var = sb("var", [P, T])
        rstd = sb("rstd", [P, T])
        wdt = sb("wdt", [P, KC, HEADS])
        small = sb("small", [P, 8, T])
        lbt = sb("lbt", [P, 6, KC])
        aexp = sb("aexp", [HEADS, 1])
        bank = [ctx.enter_context(nc.psum_tensor(f"bank{i}", [P, 512], F32)) for i in range(8)]

        flat = big[:, :, :].rearrange("p a b -> p (a b)")

        def work(at, n, m=1):
            v = flat[:, at:at + n]
            return v if m == 1 else v.rearrange("p (m n) -> p m n", m=m)

        def par_at(name, i=0, rows=P):
            a = PAR[name][0] + i
            return pars[0:rows, a:a + 1]

        def acc(m):
            return bank[4 + m // 2][:, (m % 2) * T:(m % 2 + 1) * T]

        raw_in = [sem(f"raw_in{r}") for r in range(RAW)]
        hi_done = sem("hi_done")
        lo_pool = sem("lo_pool")
        lo_dve = sem("lo_dve")
        mm_done = sem("mm_done")
        evac = sem("evac")
        x_in = sem("x_in")
        par_in = sem("par_in")
        tri_in = sem("tri_in")
        lev_in = sem("lev_in")
        keys_in = sem("keys_in")
        stored = sem("stored")
        ones_set = sem("ones_set")
        sq_done = sem("sq_done")
        ms_done = sem("ms_done")
        var_done = sem("var_done")
        sd_done = sem("sd_done")
        hn_done = sem("hn_done")
        hhi_done = sem("hhi_done")
        hlo_done = sem("hlo_done")
        x_done = sem("x_done")
        own = sem("own")
        pads = sem("pads")
        conv_step = sem("conv_step")
        conv_act = sem("conv_act")
        dt_mm = sem("dt_mm")
        dt_v = sem("dt_v")
        dt_a = sem("dt_a")
        tok_mm = sem("tok_mm")
        tok_v = sem("tok_v")
        xt_mm = sem("xt_mm")
        xt_v = sem("xt_v")
        bt_mm = sem("bt_mm")
        bt_v = sem("bt_v")
        cb_mm = sem("cb_mm")
        cb_v = sem("cb_v")
        seg_mm = sem("seg_mm")
        seg_v = sem("seg_v")
        seg_a = sem("seg_a")
        dec_a = sem("dec_a")
        dec_v = sem("dec_v")
        st_mm = sem("st_mm")
        st_a = sem("st_a")
        z_act = sem("z_act")
        y_mm = sem("y_mm")
        y_v = sem("y_v")
        ysq = sem("ysq")
        yms = sem("yms")
        yvar = sem("yvar")
        ysd = sem("ysd")
        yn = sem("yn")
        hg_a = sem("hg_a")
        hg_v = sem("hg_v")
        hset = sem("hset")
        lb_v = sem("lb_v")
        lb_a = sem("lb_a")
        it_mm = sem("it_mm")
        it_a = sem("it_a")
        lev_v = sem("lev_v")
        lev_a = sem("lev_a")
        lev_q = sem("lev_q")
        lev_mm = sem("lev_mm")
        att_v = sem("att_v")
        att_a = sem("att_a")
        o_mm = sem("o_mm")
        osq = sem("osq")
        oms = sem("oms")
        ovar = sem("ovar")
        osd = sem("osd")
        on = sem("on")
        sc_mm = sem("sc_mm")
        sc_a = sem("sc_a")
        tk = sem("tk")
        lists = sem("lists")
        gexp = sem("gexp")
        gate_v = sem("gate_v")
        lt_mm = sem("lt_mm")
        lt_v = sem("lt_v")
        oha_done = sem("oha_done")
        dif_done = sem("dif_done")
        dif_sq = sem("dif_sq")
        ohb_done = sem("ohb_done")
        gate_mm = sem("gate_mm")
        gated = sem("gated")
        chi = sem("chi")
        clo = sem("clo")

        sq = work(0, 2048, KC)
        hn = work(2048, 2048, KC)
        zs = work(0, 4096, XT)
        xc = work(4096, 6144, CONV)
        pad = work(10240, CONV * (T + 3), CONV)
        decay = work(10240, 8192).rearrange("p (c h l) -> p c h l", c=NB, h=HEADS)
        ysquare = work(10240, 4096, XT)
        yvars = work(14336, 1024, GROUPS)
        xdt = work(18432, 4096).rearrange("p (c m) -> p c m", c=NB)
        xtail = work(22528, 2048)
        cexp = work(24576, 4096, HEADS)
        state = work(28672, 2048, GROUPS)
        btok = work(30720, 512, GROUPS)
        cbm = work(31232, 1024, 2 * GROUPS)
        tok5 = work(32256, 5 * HEADS, 5)
        tri = work(32416, 128)
        b_t, c_t = xc[:, XT:XT + GROUPS, :], xc[:, XT + GROUPS:CONV, :]
        fr = work(0, 2048, KC)
        qr = work(2048, 2048, KC)
        ir = work(4096, 2048, KC)
        gr = work(6144, 2048, KC)
        kr = work(8192, 2048, KC)
        bc = work(10240, 2048, KC)
        ebuf = [work(12288, 2048, KC), work(14336, 2048, KC)]
        att = work(16384, 2048, 2 * HGRN_HEADS)
        att2 = work(18432, 1024, HGRN_HEADS)
        itok = work(19456, 2048, NB)
        on_t = work(21504, 2048, KC)
        lev = work(23552, 128 * len(LEVELS), len(LEVELS))
        reset = work(24576, 2048, KC)
        sig = work(26624, 2048, KC)
        osquare = work(28672, 2048, KC)
        ovars = work(30720, 2048, KC)
        base = SCRATCH0 * T
        q_t = work(base, 4096, 2 * PH)
        eq = work(base, 2048)
        sk = work(base + 4096, 2048, 2 * PH)
        sc = work(base + 6144, 4096).rearrange("p (b m k) -> p b m k", b=NB, m=2 * PH)
        tkw = base + 10240
        repl = work(tkw, 256, 2)
        cand = work(tkw + 256, 256)
        cand2 = work(tkw + 512, 256)
        topv = work(tkw + 768, 256).rearrange("p (h c k) -> p h c k", h=PH, c=2)
        topi = work(tkw + 1024, 256).bitcast(U32).rearrange("p (h c k) -> p h c k", h=PH, c=2)
        topf = work(tkw + 1280, 256).rearrange("p (h c k) -> p h c k", h=PH, c=2)
        pos = work(tkw + 1536, 128).bitcast(U32)
        half = work(tkw + 1664, 256, 2).bitcast(U32)
        halff = work(tkw + 1920, 256, 2)
        dif = [hhi[:, 2 * r:2 * r + 2, :].rearrange("p a (b k) -> p (a b) k", k=P) for r in range(2)]
        ohb = [hlo[:, 2 * r:2 * r + 2, :].rearrange("p a (b k) -> p (a b) k", k=P) for r in range(4)]
        lst = small

        def rounds(eng, name, body, first=True, last=False):
            n = COUNT[name] // RAW
            a, b = int(first), n - int(last)
            if first:
                body(0)
            if b > a:
                with eng.Fori(a, b) as i:
                    body(i)
            if last:
                body(n - 1)

        block = ctx.enter_context(nc.Block())

        @block.sync
        def _(sp):
            sp.dma_start(pars[:, :], par).then_inc(par_in, 16)
            sp.dma_start(x[:, :, :], x_t).then_inc(x_in, 16)
            sp.dma_start(ident[:, :], con[CON["ident"]]).then_inc(par_in, 16)
            sp.dma_start(iota[:, :], con[CON["iota"]]).then_inc(par_in, 16)
            sp.dma_start(wdt[:, :, :], w_dt).then_inc(par_in, 16)
            sp.dma_start(tri, con[CON["tri"]]).then_inc(tri_in, 16)

            def load(name, i, r, before):
                if before is not None:
                    lo, count = before
                    sp.wait_ge(lo, count)
                sp.dma_start(raw[:, r, :, :], weights[name][RAW * i + r]
                             .rearrange("p (k c) -> p k c", k=KC)).then_inc(raw_in[r], 16)

            prev = None
            for name in STAGES:
                v = name[0] == "v"
                lo, at = (lo_dve, DVE_LO) if v else (lo_pool, POOL_LO)
                if name in ("q0", "q1"):
                    sp.wait_ge(hlo_done, ACTS["y1" if name == "q0" else "hgrn_out"])
                    sp.dma_start(sk, sub_keys[int(name[1])]).then_inc(keys_in, 16)

                def body(i):
                    for r in range(RAW):
                        if isinstance(i, int) and i == 0:
                            before = None
                            if prev is not None:
                                plo, pat = (lo_dve, DVE_LO) if prev[0] == "v" else (lo_pool, POOL_LO)
                                before = plo, pat[prev] + COUNT[prev] - RAW + r + 1
                        else:
                            before = lo, at[name] + RAW * i + r - RAW + 1
                        load(name, i, r, before)
                if name == "hgrn_in":
                    body(0)
                    sp.wait_ge(x_done, 2)
                    sp.dma_start(lev, con[CON["lev"]:NCON].rearrange("n p q -> p n q")).then_inc(lev_in, 16)
                    with sp.Fori(1, COUNT[name] // RAW) as i:
                        body(i)
                else:
                    rounds(sp, name, body)
                prev = name
            sp.wait_ge(hn_done, 5)
            sp.dma_start(out_t, hn).then_inc(stored, 16)
            sp.wait_ge(stored, 16)

        @block.gpsimd
        def _(pool):
            nc.gpsimd.memset(pad[:, :, 0:3], 0.0).then_inc(pads, 1)

            def lo(name, i, r):
                g = FIRST[name] + RAW * i + r
                pool.wait_ge(hi_done, g + 1)
                nc.gpsimd.tensor_tensor(wlo[:, r, :, :], raw[:, r, :, :], whi[:, r, :, :].bitcast(F32),
                                        ALU.subtract).then_inc(lo_pool, 1)

            def los(name):
                with pool.Fori(0, COUNT[name] // RAW) as i:
                    for r in range(RAW):
                        lo(name, i, r)

            for layer in range(2):
                if layer == 0:
                    los("ssd_in")
                    los("ssd_out")
                else:
                    los("hgrn_in")
                    pool.wait_ge(x_done, 2)
                    nc.gpsimd.memset(reset, 1.0).then_inc(hset, 1)
                    nc.gpsimd.memset(att, 0.0).then_inc(hset, 1)
                    pool.wait_ge(hset, 2)
                    nc.gpsimd.memset(reset.rearrange("p h (c l) -> p (h c) l", l=HCHUNK)[:, :, 0:1],
                                     0.0).then_inc(hset, 1)
                    los("hgrn_out")
                los(f"q{layer}")
                los(f"u{layer}")

                pool.wait_ge(lt_v, layer + 1)

                def differences(i):
                    for q in range(4):
                        if not (isinstance(i, int) and i == 0 and q < 2 and layer == 0):
                            pool.wait_ge(ohb_done, 64 * layer + 4 * i + q - 1)
                        n = 16 * i + 4 * q
                        nc.gpsimd.tensor_tensor(dif[q % 2], iota[:, :].unsqueeze(1).to_broadcast([P, 4, P]),
                                                picks[:, 1, bass.ds(n, 4)].unsqueeze(2).to_broadcast([P, 4, P]),
                                                ALU.subtract).then_inc(dif_done, 1)
                differences(0)
                with pool.Fori(1, 16) as i:
                    differences(i)

                name = f"v{layer}"

                def c_lo(i):
                    for r in range(RAW):
                        j = RAW * i + r
                        pool.wait_ge(chi, 128 * layer + j + 1)
                        nc.gpsimd.tensor_tensor(hlo[:, r, :], big[:, bass.ds(j, 1), :].rearrange("p a b -> p (a b)"),
                                                hhi[:, r, :].bitcast(F32), ALU.subtract).then_inc(clo, 1)
                with pool.Fori(0, 32) as i:
                    c_lo(i)

        @block.scalar
        def _(act):
            def hi(g, r):
                act.wait_ge(raw_in[r], 16 * (g // RAW + 1) if isinstance(g, int) else 4 * (g - r) + 16)
                if not isinstance(g, int) or g >= SPL:
                    act.wait_ge(mm_done, g - SPL + 1)
                nc.scalar.activation(whi[:, r, :, :], raw[:, r, :, :], ACT.Copy).then_inc(hi_done, 1)

            def stream(name, out, a=0, b=None, last=False):
                def body(i, end=False):
                    for r in range(RAW):
                        g = FIRST[name] + RAW * i + r
                        if not end or r < 2:
                            hi(g + 2, (r + 2) % RAW)
                        out(RAW * i + r, r, g)
                b = COUNT[name] // RAW if b is None else b
                if a == 0 and name == "ssd_in":
                    body(0)
                    a = 1
                if b - int(last) > a:
                    with act.Fori(a, b - int(last)) as i:
                        body(i)
                if last:
                    body(b - 1, end=True)

            def copy_to(dst):
                def out(t, r, g):
                    act.wait_ge(mm_done, g + 1)
                    nc.scalar.activation(dst(t), bank[r][:, 0:T], ACT.Copy).then_inc(evac, 1)
                return out

            def col(t):
                return big[:, bass.ds(t, 1), :].rearrange("p a b -> p (a b)")

            def norm(n, ready, value):
                act.wait_ge(ready, value)
                nc.scalar.activation(sq, x[:, :, :], ACT.Square).then_inc(sq_done, 1)
                act.wait_ge(var_done, n + 1)
                nc.scalar.activation(rstd[:, :], var[:, :], ACT.Sqrt).then_inc(sd_done, 1)

            def acts_hi(src, ready, value):
                act.wait_ge(ready, value)
                nc.scalar.activation(hhi[:, :, :], src, ACT.Copy).then_inc(hhi_done, 1)

            hi(0, 0)
            hi(1, 1)
            norm(0, x_in, 16)
            acts_hi(hn, hn_done, 1)
            act.wait_ge(par_in, 64)
            act.wait_ge(dt_v, 1)
            nc.scalar.activation(small[0:HEADS, 1, :], small[0:HEADS, 1, :], ACT.Exp).then_inc(dt_a, 1)
            nc.scalar.activation(aexp[:, :], par_at("a_log", 0, HEADS), ACT.Exp).then_inc(dt_a, 1)
            act.wait_ge(lb_v, 1)
            nc.scalar.activation(lbt[:, 0:2, :], lbt[:, 0:2, :], ACT.Exp).then_inc(lb_a, 1)
            act.wait_ge(dt_v, 2)
            nc.scalar.activation(small[0:HEADS, 3, :], small[0:HEADS, 2, :], ACT.Ln).then_inc(dt_a, 1)
            act.wait_ge(dt_v, 3)
            nc.scalar.activation(small[0:HEADS, 3, 0:P], small[0:HEADS, 3, 0:P], ACT.Exp).then_inc(dt_a, 1)
            nc.scalar.preload_act_table(ACT.Silu)

            def to_pad(t):
                return pad[:, bass.ds(t, 1), 3:T + 3].rearrange("p a b -> p (a b)")

            def conv_silu(i):
                act.wait_ge(conv_step, 16 * i + 16)
                v = xc[:, bass.ds(4 * i, 4), :]
                nc.scalar.activation(v, v, ACT.Silu).then_inc(conv_act, 1)

            stream("ssd_in", copy_to(to_pad), 0, CONV // RAW)
            for q in range(CONV // 4 - 2):
                conv_silu(q)
            stream("ssd_in", copy_to(lambda t: col(t - CONV)), CONV // RAW)
            for q in range(CONV // 4 - 2, CONV // 4):
                conv_silu(q)
            act.wait_ge(evac, SSD_TILES)
            nc.scalar.activation(zs, zs, ACT.Silu).then_inc(z_act, 1)
            for q in range(HEADS // 2):
                act.wait_ge(seg_v, q + 1)
                src = bank[q % 4][:, :].rearrange("p (h t) -> p h t", h=2)[:, :, P:T]
                nc.scalar.activation(cexp[:, 2 * q:2 * q + 2, :], src, ACT.Exp).then_inc(seg_a, 1)
                if q % 4 == 3:
                    g = q // 4
                    for c in range(NB):
                        v = decay[:, c, 8 * g:8 * g + 8, :]
                        nc.scalar.activation(v, v, ACT.Exp).then_inc(dec_a, 1)
            act.wait_ge(st_mm, 1)
            for g in range(GROUPS):
                nc.scalar.activation(state[:, g, :], bank[4 + g][:, :], ACT.Copy).then_inc(st_a, 1)
            for g in range(GROUPS):
                act.wait_ge(y_v, g + 1)
                nc.scalar.activation(ysquare[:, 4 * g:4 * g + 4, :], xc[:, 4 * g:4 * g + 4, :],
                                     ACT.Square).then_inc(ysq, 1)
            act.wait_ge(yvar, 1)
            nc.scalar.activation(yvars, yvars, ACT.Sqrt).then_inc(ysd, 1)
            acts_hi(xc[:, 0:KC, :], yn, 1)
            with act.Fori(0, 2) as i:
                for r in range(RAW):
                    hi(FIRST["ssd_out"] + RAW * i + r + 2, (r + 2) % RAW)
            act.wait_ge(mm_done, FIRST["ssd_out"] + KC)
            acts_hi(xc[:, KC:XT, :], yn, 1)
            with act.Fori(2, 4) as i:
                for r in range(RAW):
                    hi(FIRST["ssd_out"] + RAW * i + r + 2, (r + 2) % RAW)

            for layer in range(2):
                if layer == 1:
                    norm(2, x_done, 2)
                    acts_hi(hn, hn_done, 3)
                    stream("hgrn_in", copy_to(col))
                    act.wait_ge(evac, EVAC["hgrn_out"])
                    nc.scalar.activation(sig, fr, ACT.Sigmoid).then_inc(hg_a, 1)
                    nc.scalar.activation(kr, fr, ACT.Sigmoid, scale=-1.0).then_inc(hg_a, 1)
                    nc.scalar.activation(gr, gr, ACT.Silu).then_inc(hg_a, 1)
                    act.wait_ge(hg_v, 1)
                    nc.scalar.activation(fr, sig, ACT.Ln).then_inc(hg_a, 1)
                    for b in range(NB * 2):
                        act.wait_ge(it_mm, b + 1)
                        nc.scalar.activation(itok[:, b // 2, 512 * (b % 2):512 * (b % 2) + 512],
                                             bank[b][:, :], ACT.Copy).then_inc(it_a, 1)
                    for n in range(len(LEVELS) + 1):
                        act.wait_ge(lev_v, n + 1)
                        nc.scalar.activation(ebuf[n % 2], ebuf[n % 2], ACT.Exp).then_inc(lev_a, 1)
                    act.wait_ge(lev_mm, len(LEVELS) + 2)
                    n = len(LEVELS) + 1
                    for b in range(2):
                        nc.scalar.activation(att2[:, 4 * b:4 * b + 4, :],
                                             bank[4 * (n % 2) + b][:, :].rearrange("p (h l) -> p h l", h=4),
                                             ACT.Copy).then_inc(att_a, 1)
                    for b in range(4):
                        act.wait_ge(o_mm, b + 1)
                        nc.scalar.activation(osquare[:, 2 * b:2 * b + 2, :],
                                             bank[b][:, :].rearrange("p (h l) -> p h l", h=2),
                                             ACT.Square).then_inc(osq, 1)
                    act.wait_ge(ovar, 4)
                    nc.scalar.activation(ovars, ovars, ACT.Sqrt).then_inc(osd, 1)
                    acts_hi(on_t, on, 1)
                    with act.Fori(0, 2) as i:
                        for r in range(RAW):
                            hi(FIRST["hgrn_out"] + RAW * i + r + 2, (r + 2) % RAW)

                if layer == 0:
                    norm(1, x_done, 1)
                else:
                    norm(3, evac, EVAC["q1"])
                acts_hi(hn, hn_done, 2 * layer + 2)
                stream(f"q{layer}", copy_to(lambda t: col(t + SCRATCH0)))
                for n in range(2 * 4):
                    act.wait_ge(sc_mm, 8 * layer + n + 1)
                    b, m = divmod(n, 4)
                    nc.scalar.activation(sc[:, b, 4 * m:4 * m + 4, :],
                                         bank[4 + n % 4][:, :].rearrange("p (m k) -> p m k", m=4),
                                         ACT.Copy).then_inc(sc_a, 1)
                nc.scalar.preload_act_table(ACT.Gelu)

                def gelu(t, r, g):
                    act.wait_ge(mm_done, g + 1)
                    nc.scalar.activation(col(t), bank[r][:, 0:T], ACT.Gelu).then_inc(evac, 1)
                stream(f"u{layer}", gelu, 0, SCRATCH0 // RAW)
                act.wait_ge(lists, 2 * layer + 2)
                stream(f"u{layer}", gelu, SCRATCH0 // RAW)
                nc.scalar.activation(lst[:, 2, :], lst[:, 2, :], ACT.Exp).then_inc(gexp, 1)

                def one_hots(i):
                    for q in range(4):
                        n = 64 * layer + 4 * i + q
                        act.wait_ge(dif_done, n + 1)
                        v = dif[q % 2]
                        nc.scalar.activation(v, v.bitcast(F32), ACT.Square).then_inc(dif_sq, 1)
                        if not (isinstance(i, int) and i == 0 and layer == 0):
                            act.wait_ge(gate_mm, n - 3)
                        act.wait_ge(dif_sq, n + 1)
                        nc.scalar.activation(ohb[q], v.bitcast(F32), ACT.Relu, bias=1.0,
                                             scale=-1.0).then_inc(ohb_done, 1)
                one_hots(0)
                with act.Fori(1, 16) as i:
                    one_hots(i)

                def c_hi(j, r):
                    nc.scalar.activation(hhi[:, r, :], col(j), ACT.Copy).then_inc(chi, 1)
                act.wait_ge(gated, 64 * layer + 64)
                name = f"v{layer}"
                c_hi(0, 0)
                c_hi(1, 1)

                def v_round(i, end=False):
                    for r in range(RAW):
                        g = FIRST[name] + RAW * i + r
                        last = layer == 1
                        if not (end and r >= 2 and last):
                            hi(g + 2, (r + 2) % RAW)
                        if not (end and r >= 2):
                            act.wait_ge(mm_done, g + 2 - RAW + 1)
                            c_hi(RAW * i + r + 2, (r + 2) % RAW)
                with act.Fori(0, COUNT[name] // RAW - 1) as i:
                    v_round(i)
                v_round(COUNT[name] // RAW - 1, end=True)
            norm(4, x_done, 3)

        @block.tensor
        def _(pe):
            def split(out, r, start, stop, **kw):
                n = 0
                for k in range(KC):
                    for w, h in ((whi, hhi), (whi, hlo), (wlo, hhi)):
                        ins = nc.tensor.matmul(out, w[:, r, k, :], h[:, k, :], start=start and n == 0,
                                               stop=stop and n == 3 * KC - 1, **kw)
                        n += 1
                return ins

            def tile_ready(name, i, r):
                g = FIRST[name] + RAW * i + r
                pe.wait_ge(hi_done, g + 1)
                if name[0] == "v":
                    pe.wait_ge(lo_dve, DVE_LO[name] + RAW * i + r + 1)
                else:
                    pe.wait_ge(lo_pool, POOL_LO[name] + RAW * i + r + 1)

            def project(name):
                def body(i):
                    for r in range(RAW):
                        tile_ready(name, i, r)
                        e = EVAC[name] + RAW * i + r
                        if not isinstance(e, int) or e >= BANKS:
                            pe.wait_ge(evac, e - BANKS + 1)
                        split(bank[r][:, 0:T], r, True, True).then_inc(mm_done, 1)
                rounds(pe, name, body, first=EVAC[name] == 0)

            def clear():
                for b in range(4, 8):
                    nc.tensor.matmul(bank[b][:, :], zero[:, 0:P], zero[:, :], start=True, stop=True,
                                     skip_group_check=True)

            def acts(name):
                pe.wait_ge(hhi_done, ACTS[name])
                pe.wait_ge(hlo_done, ACTS[name])

            def norm(n):
                pe.wait_ge(sq_done, n + 1)
                for k in range(KC):
                    ins = nc.tensor.matmul(bank[7][:, 0:T], ones[:, :], sq[:, k, :], start=k == 0,
                                           stop=k == KC - 1)
                ins.then_inc(ms_done, 1)

            pe.wait_ge(ones_set, 2)
            norm(0)
            pe.wait_ge(hn_done, 1)
            pe.wait_ge(par_in, 64)
            for k in range(KC):
                ins = nc.tensor.matmul(bank[4][0:HEADS, 0:T], wdt[:, k, :], hn[:, k, :], start=k == 0,
                                       stop=k == KC - 1)
            ins.then_inc(dt_mm, 1)
            acts("ssd_in")
            project("ssd_in")
            pe.wait_ge(dt_v, 4)
            idn = ident[0:HEADS, 0:HEADS]
            for n, (slot, c) in enumerate([(6, 0), (6, 1), (7, 0), (7, 1), (3, 0)]):
                ins = nc.tensor.transpose(bank[4][:, T + HEADS * n:T + HEADS * (n + 1)],
                                          small[0:HEADS, slot, c * P:(c + 1) * P], idn)
            ins.then_inc(tok_mm, 1)
            pe.wait_ge(conv_act, CONV // 4)
            pe.wait_ge(evac, SSD_TILES)
            for n in range(8):
                c, q = divmod(n, 4)
                b = (0, 1, 2, 3, 5, 6, 7, 0)[n]
                if n == 7:
                    pe.wait_ge(xt_v, 1)
                for m in range(4):
                    ins = nc.tensor.transpose(bank[b][:, P * m:P * (m + 1)],
                                              xc[:, 4 * q + m, c * P:(c + 1) * P], ident[:, :])
                ins.then_inc(xt_mm, 1)
            pe.wait_ge(tok_v, 1)
            for g in range(GROUPS):
                ins = nc.tensor.transpose(bank[4][:, P * g:P * (g + 1)], b_t[:, g, 0:P], ident[:, :])
            ins.then_inc(bt_mm, 1)
            for c in range(NB):
                pe.wait_ge(xt_v, 5 + c)
                for g in range(GROUPS):
                    t = slice(c * P, (c + 1) * P)
                    ins = nc.tensor.matmul(bank[5 + c][:, P * g:P * (g + 1)], b_t[:, g, t], c_t[:, g, t],
                                           start=True, stop=True)
                ins.then_inc(cb_mm, 1)
            pe.wait_ge(xt_v, 8)
            for q in range(HEADS // 2):
                if q >= 4:
                    pe.wait_ge(seg_v, q - 3)
                    pe.wait_ge(seg_a, q - 3)
                for e in range(2):
                    h = 2 * q + e
                    ins = nc.tensor.matmul(bank[q % 4][:, e * T:(e + 1) * T],
                                           ident[0:HEADS, h:h + 1].to_broadcast([HEADS, P]),
                                           small[0:HEADS, 7, :], start=True, stop=True)
                ins.then_inc(seg_mm, 1)
            pe.wait_ge(bt_v, 1)
            pe.wait_ge(cb_v, 2)
            for g in range(GROUPS):
                ins = nc.tensor.matmul(bank[4 + g][:, :], btok[:, g, :], xtail[:, 512 * g:512 * (g + 1)],
                                       start=True, stop=True)
            ins.then_inc(st_mm, 1)
            pe.wait_ge(seg_v, 16)
            pe.wait_ge(seg_a, 16)
            pe.wait_ge(st_a, GROUPS)
            for n in range(XT // 2):
                if n % 2 == 0:
                    pe.wait_ge(dec_v, 3 * (n // 2) + 3)
                for e in range(2):
                    m = 2 * n + e
                    for hh in range(2):
                        h = 2 * m + hh
                        rows = slice(64 * hh, 64 * hh + 64)
                        for c in range(NB):
                            out = bank[n % 8][rows, e * T + c * P:e * T + (c + 1) * P]
                            nc_in = nc.tensor.matmul(out, xdt[:, c, 64 * h:64 * h + 64], decay[:, c, h, :],
                                                     start=True, stop=c == 0)
                            if c == 1:
                                hg = 64 * (h % 8)
                                nc_in = nc.tensor.matmul(out, state[:, h // 8, hg:hg + 64], cexp[:, h, :],
                                                         start=False, stop=True)
                nc_in.then_inc(y_mm, 1)
            for g in range(GROUPS):
                pe.wait_ge(ysq, g + 1)
                for m in range(4):
                    ins = nc.tensor.matmul(bank[g // 2][:, (g % 2) * T:(g % 2 + 1) * T], ones[:, :],
                                           ysquare[:, 4 * g + m, :], start=m == 0, stop=m == 3)
                ins.then_inc(yms, 1)
            pe.wait_ge(y_v, 4)
            clear()

            def accumulate(name, i, half):
                for r in range(RAW):
                    m = RAW * (i % 2) + r
                    tile_ready(name, i, r)
                    split(acc(m), r, False, True, skip_group_check=True).then_inc(mm_done, 1)
            for i in range(4):
                if i % 2 == 0:
                    acts(f"y{i // 2}")
                accumulate("ssd_out", i, i // 2)

            for layer in range(2):
                if layer == 1:
                    norm(2)
                    acts("hgrn_in")
                    project("hgrn_in")
                    pe.wait_ge(evac, EVAC["hgrn_out"])
                    for n in range(4):
                        b, part = divmod(n, 2)
                        for m in range(4):
                            ins = nc.tensor.transpose(bank[n][:, P * m:P * (m + 1)],
                                                      ir[:, 4 * part + m, b * P:(b + 1) * P], ident[:, :])
                        ins.then_inc(it_mm, 1)
                    pe.wait_ge(it_a, 4)
                    for n in range(len(LEVELS) + 2):
                        if n == 0:
                            pe.wait_ge(hg_v, 3)
                            kk, qq = kr, qr
                        else:
                            pe.wait_ge(lev_q, n)
                            kk = qq = ebuf[(n - 1) % 2]
                        if n >= 2:
                            pe.wait_ge(att_v, 4 * (n - 1))
                        for b in range(4):
                            if n == len(LEVELS) + 1 and b >= 2:
                                break
                            for m in range(4):
                                if n <= len(LEVELS):
                                    h, blk = divmod(4 * b + m, 2)
                                    ks = qs = slice(blk * P, (blk + 1) * P)
                                else:
                                    h, ks, qs = 4 * b + m, slice(0, P), slice(P, T)
                                ins = nc.tensor.matmul(bank[4 * (n % 2) + b][:, P * m:P * (m + 1)],
                                                       kk[:, h, ks], qq[:, h, qs], start=True, stop=True)
                        ins.then_inc(lev_mm, 1)
                    pe.wait_ge(att_v, 4 * (len(LEVELS) + 1))
                    pe.wait_ge(att_a, 2)
                    for b in range(4):
                        for e in range(2):
                            h = 2 * b + e
                            v = slice(P * h, P * h + P)
                            o0 = bank[b][:, e * T:e * T + P]
                            o1 = bank[b][:, e * T + P:(e + 1) * T]
                            nc.tensor.matmul(o0, itok[:, 0, v], att[:, 2 * h, :], start=True, stop=True)
                            nc.tensor.matmul(o1, itok[:, 1, v], att[:, 2 * h + 1, :], start=True, stop=False)
                            ins = nc.tensor.matmul(o1, itok[:, 0, v], att2[:, h, :], start=False, stop=True)
                        ins.then_inc(o_mm, 1)
                    for b in range(4):
                        pe.wait_ge(osq, b + 1)
                        nc.tensor.matmul(bank[4 + b][:, :], ones[:, :],
                                         osquare[:, 2 * b:2 * b + 2, :].rearrange("p h l -> p (h l)"),
                                         start=True, stop=True).then_inc(oms, 1)
                    acts("hgrn_out")
                    project("hgrn_out")

                norm(1 + 2 * layer)
                acts(f"q{layer}")
                project(f"q{layer}")
                pe.wait_ge(keys_in, 16 * layer + 16)
                pe.wait_ge(evac, EVAC[f"u{layer}"])
                for n in range(8):
                    if n >= 4:
                        pe.wait_ge(sc_a, 8 * layer + n - 3)
                    b, q = divmod(n, 4)
                    for m in range(4):
                        ins = nc.tensor.matmul(bank[4 + n % 4][:, P * m:P * (m + 1)],
                                               q_t[:, 4 * q + m, b * P:(b + 1) * P], sk[:, 4 * q + m, :],
                                               start=True, stop=True)
                    ins.then_inc(sc_mm, 1)
                project(f"u{layer}")
                pe.wait_ge(sc_a, 8 * layer + 8)
                for n in range(6):
                    kind, b = divmod(n, 2)
                    if n == 4:
                        pe.wait_ge(gate_v, layer + 1)
                    ins = nc.tensor.transpose(bank[4 + n // 4][:, P * (n % 4):P * (n % 4 + 1)],
                                              lst[:, kind, b * P:(b + 1) * P], ident[:, :])
                ins.then_inc(lt_mm, 1)

                pe.wait_ge(evac, EVAC[f"u{layer}"] + 128)

                def gates(i):
                    for q in range(4):
                        n = 64 * layer + 4 * i + q
                        pe.wait_ge(oha_done, n + 1)
                        pe.wait_ge(ohb_done, n + 1)
                        if not (isinstance(i, int) and i == 0 and layer == 0):
                            pe.wait_ge(gated, n - 3)
                        for t in range(4):
                            ins = nc.tensor.matmul(bank[q][:, P * t:P * (t + 1)], oha[:, q % 2, t, :],
                                                   ohb[q][:, t, :].bitcast(F32), start=True, stop=True)
                        ins.then_inc(gate_mm, 1)
                gates(0)
                with pe.Fori(1, 16) as i:
                    gates(i)

                pe.wait_ge(lt_v, layer + 1)
                clear()
                name = f"v{layer}"

                def contract(i):
                    for r in range(RAW):
                        tile_ready(name, i, r)
                        pe.wait_ge(chi, 128 * layer + RAW * i + r + 1)
                        pe.wait_ge(clo, 128 * layer + RAW * i + r + 1)
                        for m in range(KC):
                            for w, h in ((whi, hhi), (whi, hlo), (wlo, hhi)):
                                ins = nc.tensor.matmul(acc(m), w[:, r, m, :], h[:, r, :], start=False,
                                                       stop=True, skip_group_check=True)
                        ins.then_inc(mm_done, 1)
                with pe.Fori(0, 32) as i:
                    contract(i)
            norm(4)

        @block.vector
        def _(dve):
            count = [0]

            def step(ins):
                count[0] += 1
                ins.then_inc(own, 1)
                dve.wait_ge(own, count[0])

            def norm(n, split=True):
                dve.wait_ge(ms_done, n + 1)
                nc.vector.tensor_scalar(var[:, :], bank[7][:, 0:T], EPS, None, ALU.add).then_inc(var_done, 1)
                dve.wait_ge(sd_done, n + 1)
                step(nc.vector.reciprocal(rstd[:, :], rstd[:, :]))
                for k in range(KC):
                    ins = nc.vector.scalar_tensor_tensor(out=hn[:, k, :], in0=x[:, k, :],
                                                         scalar=par_at("norm_g", n * KC + k),
                                                         in1=rstd[:, :], op0=ALU.mult, op1=ALU.mult)
                ins.then_inc(hn_done, 1)

            def acts_lo(src, value):
                dve.wait_ge(hhi_done, value)
                nc.vector.tensor_tensor(hlo[:, :, :], src, hhi[:, :, :].bitcast(F32),
                                        ALU.subtract).then_inc(hlo_done, 1)

            def add_acc(value):
                dve.wait_ge(mm_done, value)
                for b in range(4):
                    v = x[:, 2 * b:2 * b + 2, :]
                    ins = nc.vector.tensor_tensor(v, v, bank[4 + b][:, :].rearrange("p (m t) -> p m t", m=2),
                                                  ALU.add)
                ins.then_inc(x_done, 1)

            nc.vector.memset(ones[:, :], 1.0 / D).then_inc(ones_set, 1)
            nc.vector.memset(zero[:, :], 0.0).then_inc(ones_set, 1)
            dve.wait_ge(par_in, 64)
            a = PAR["lb"][0]
            lg = pars[:, a:a + 2 * KC].rearrange("p (l k) -> p l k", l=2)
            step(nc.vector.tensor_tensor(lbt[:, 2, :], lg[:, 0, :], lg[:, 1, :], ALU.max))
            nc.vector.tensor_tensor(lbt[:, 0:2, :], lg, lbt[:, 2:3, :].to_broadcast([P, 2, KC]),
                                    ALU.subtract).then_inc(lb_v, 1)

            norm(0)
            dve.wait_ge(dt_mm, 1)
            sm = lambda i: small[0:HEADS, i, :]
            v, u, w, t3, d, z, dt, acs = (sm(i) for i in range(8))
            step(nc.vector.tensor_scalar(v, bank[4][0:HEADS, 0:T], par_at("dt_bias", 0, HEADS), None, ALU.add))
            step(nc.vector.tensor_scalar(u, v, -1.0, None, ALU.mult))
            nc.vector.tensor_tensor(u, u, v, ALU.min).then_inc(dt_v, 1)
            acts_lo(hn, ACTS["ssd_in"])
            dve.wait_ge(dt_a, 2)
            nc.vector.tensor_scalar(w, u, 1.0, None, ALU.add).then_inc(dt_v, 1)
            dve.wait_ge(dt_v, 2)
            step(nc.vector.tensor_scalar(d, w, -1.0, None, ALU.add))
            step(nc.vector.tensor_scalar(z, d, 0.0, None, ALU.is_equal))
            step(nc.vector.tensor_tensor(d, d, z, ALU.add))
            step(nc.vector.reciprocal(d, d))
            step(nc.vector.tensor_tensor(z, z, u, ALU.mult))
            dve.wait_ge(dt_a, 3)
            step(nc.vector.tensor_tensor(t3, t3, u, ALU.mult))
            step(nc.vector.tensor_tensor(t3, t3, d, ALU.mult))
            step(nc.vector.tensor_tensor(t3, t3, z, ALU.add))
            step(nc.vector.scalar_tensor_tensor(out=dt, in0=v, scalar=0.0, in1=t3, op0=ALU.max, op1=ALU.add))
            step(nc.vector.tensor_scalar(d, dt, aexp[:, :], -1.0, ALU.mult, ALU.mult))
            step(nc.vector.memset(z, 1.0))
            step(nc.vector.memset(z.rearrange("p (c l) -> p c l", l=P)[:, :, 0:1], 0.0))
            step(nc.vector.tensor_tensor_scan(acs, z, d, 0.0, ALU.mult, ALU.add))
            nc.vector.tensor_scalar(t3[:, 0:P], acs[:, 0:P], -1.0, acs[:, P - 1:P], ALU.mult,
                                    ALU.add).then_inc(dt_v, 1)
            dve.wait_ge(dt_a, 4)
            nc.vector.tensor_tensor(t3[:, 0:P], t3[:, 0:P], dt[:, 0:P], ALU.mult).then_inc(dt_v, 1)
            dve.wait_ge(lb_a, 1)
            step(nc.vector.tensor_tensor(lbt[:, 2, :], lbt[:, 0, :], lbt[:, 1, :], ALU.add))
            step(nc.vector.reciprocal(lbt[:, 2, :], lbt[:, 2, :]))
            step(nc.vector.tensor_tensor(lbt[:, 0:2, :], lbt[:, 0:2, :],
                                         lbt[:, 2:3, :].to_broadcast([P, 2, KC]), ALU.mult))
            step(nc.vector.tensor_tensor(lbt[:, 3, :], lbt[:, 0, :], lbt[:, 1, :], ALU.add))
            step(nc.vector.tensor_tensor(lbt[:, 3, :], lbt[:, 3, :], lbt[:, 0, :], ALU.subtract))
            step(nc.vector.tensor_scalar(lbt[:, 4, :], lbt[:, 3, :], -1.0, 1.0, ALU.mult, ALU.add))
            dve.wait_ge(pads, 1)
            for i in range(CONV // 4):
                dve.wait_ge(evac, 4 * i + 4)
                for tap in range(4):
                    if tap:
                        dve.wait_ge(conv_step, 16 * i + 4 * tap)
                    for m in range(4 * i, 4 * i + 4):
                        src = pad[:, m, 3 - tap:3 - tap + T]
                        cw = par_at("conv_w", 4 * m + 3 - tap)
                        if tap == 0:
                            ins = nc.vector.tensor_scalar(xc[:, m, :], src, cw, par_at("conv_b", m),
                                                          ALU.mult, ALU.add)
                        else:
                            ins = nc.vector.scalar_tensor_tensor(out=xc[:, m, :], in0=src, scalar=cw,
                                                                 in1=xc[:, m, :], op0=ALU.mult, op1=ALU.add)
                        ins.then_inc(conv_step, 1)
            dve.wait_ge(tok_mm, 1)
            nc.vector.tensor_copy(tok5, bank[4][:, T:T + 5 * HEADS].rearrange("p (n h) -> p n h", n=5)) \
                .then_inc(tok_v, 1)
            dve.wait_ge(tok_v, 1)
            for n in range(8):
                c, q = divmod(n, 4)
                b = (0, 1, 2, 3, 5, 6, 7, 0)[n]
                dve.wait_ge(xt_mm, n + 1)
                src = bank[b][:, :].rearrange("p (h v) -> p h v", h=8)
                outs = [(xdt[:, c, 512 * q:512 * (q + 1)], c)] + [(xtail[:, 512 * q:512 * (q + 1)], 4)] * (c == 0)
                for out, slot in outs:
                    by = tok5[:, slot, 8 * q:8 * q + 8].unsqueeze(2).to_broadcast([P, 8, 64])
                    ins = nc.vector.tensor_tensor(out.rearrange("p (h v) -> p h v", h=8), src, by, ALU.mult)
                ins.then_inc(xt_v, 1)
            dve.wait_ge(bt_mm, 1)
            nc.vector.tensor_copy(btok, bank[4][:, :].rearrange("p (g n) -> p g n", g=GROUPS)).then_inc(bt_v, 1)
            dve.wait_ge(tri_in, 16)
            for c in range(NB):
                dve.wait_ge(cb_mm, c + 1)
                nc.vector.tensor_tensor(cbm[:, 4 * c:4 * c + 4, :],
                                        bank[5 + c][:, :].rearrange("p (g l) -> p g l", g=GROUPS),
                                        tri.unsqueeze(1).to_broadcast([P, GROUPS, P]), ALU.mult) \
                    .then_inc(cb_v, 1)
            for q in range(HEADS // 2):
                dve.wait_ge(seg_mm, q + 1)
                for e in range(2):
                    h = 2 * q + e
                    for c in range(NB):
                        ins = nc.vector.tensor_scalar(decay[:, c, h, :],
                                                      bank[q % 4][:, e * T + c * P:e * T + (c + 1) * P],
                                                      tok5[:, 2 + c, h:h + 1], 0.0, ALU.subtract, ALU.min)
                ins.then_inc(seg_v, 1)
            dve.wait_ge(cb_v, 2)
            for g in range(GROUPS):
                hs = slice(8 * g, 8 * g + 8)
                dve.wait_ge(dec_a, 2 * g + 2)
                for c in range(NB):
                    v = decay[:, c, hs, :]
                    nc.vector.tensor_tensor(v, v, cbm[:, 4 * c + g, :].unsqueeze(1).to_broadcast([P, 8, P]),
                                            ALU.mult).then_inc(dec_v, 1)
                v = cexp[:, hs, :]
                nc.vector.tensor_tensor(v, v, c_t[:, g, P:T].unsqueeze(1).to_broadcast([P, 8, P]),
                                        ALU.mult).then_inc(dec_v, 1)
            for n in range(XT // 2):
                dve.wait_ge(y_mm, n + 1)
                for e in range(2):
                    m = 2 * n + e
                    ins = nc.vector.scalar_tensor_tensor(out=xc[:, m, :], in0=xc[:, m, :],
                                                         scalar=par_at("d_skip", m),
                                                         in1=bank[n % 8][:, e * T:(e + 1) * T],
                                                         op0=ALU.mult, op1=ALU.add)
                if n % 2:
                    step(ins)
                    if n == 1:
                        dve.wait_ge(z_act, 1)
                    if n == 1:
                        dve.wait_ge(y_mm, XT // 2)
                    v = xc[:, 2 * n - 2:2 * n + 2, :]
                    nc.vector.tensor_tensor(v, v, zs[:, 2 * n - 2:2 * n + 2, :], ALU.mult).then_inc(y_v, 1)
            dve.wait_ge(yms, 4)
            for b in range(2):
                ins = nc.vector.tensor_scalar(yvars[:, 2 * b:2 * b + 2, :],
                                              bank[b][:, :].rearrange("p (g t) -> p g t", g=2),
                                              float(D) / 512, EPS, ALU.mult, ALU.add)
            ins.then_inc(yvar, 1)
            dve.wait_ge(ysd, 1)
            step(nc.vector.reciprocal(yvars, yvars))
            for m in range(XT):
                ins = nc.vector.scalar_tensor_tensor(out=xc[:, m, :], in0=xc[:, m, :],
                                                     scalar=par_at("ssd_g", m), in1=yvars[:, m // 4, :],
                                                     op0=ALU.mult, op1=ALU.mult)
            ins.then_inc(yn, 1)
            dve.wait_ge(yn, 1)
            acts_lo(xc[:, 0:KC, :], ACTS["y0"])
            acts_lo(xc[:, KC:XT, :], ACTS["y1"])
            add_acc(FIRST["q0"])

            for layer in range(2):
                if layer == 1:
                    norm(2)
                    acts_lo(hn, ACTS["hgrn_in"])
                    dve.wait_ge(hg_a, 2)
                    for h in range(HGRN_HEADS):
                        ins = nc.vector.tensor_scalar(sig[:, h, :], sig[:, h, :], lbt[:, 4, h:h + 1],
                                                      lbt[:, 3, h:h + 1], ALU.mult, ALU.add)
                    ins.then_inc(hg_v, 1)
                    for h in range(HGRN_HEADS):
                        ins = nc.vector.tensor_scalar(kr[:, h, :], kr[:, h, :], lbt[:, 4, h:h + 1], None,
                                                      ALU.mult)
                    ins.then_inc(hg_v, 1)
                    dve.wait_ge(hg_a, 4)
                    dve.wait_ge(hset, 3)
                    nc.vector.tensor_tensor_scan(bc.rearrange("p h l -> p (h l)"),
                                                 reset.rearrange("p h l -> p (h l)"),
                                                 fr.rearrange("p h l -> p (h l)"), 0.0,
                                                 ALU.mult, ALU.add).then_inc(hg_v, 1)
                    dve.wait_ge(hg_v, 3)
                    dve.wait_ge(lev_in, 16)

                    def halves(v, m):
                        w = v.rearrange("p h l -> p (h l)").rearrange("p (n l) -> p n l", l=2 * m)
                        return w[:, :, 0:m], w[:, :, m:2 * m]

                    def exponents(n):
                        if n >= 2:
                            dve.wait_ge(lev_mm, n)
                        e = ebuf[n % 2]
                        if n < len(LEVELS) - 1:
                            m = LEVELS[n]
                            (el, eu), (bl, bu) = halves(e, m), halves(bc, m)
                            mid = bl[:, :, m - 1:m].to_broadcast([P, 2048 // (2 * m), m])
                            nc.vector.tensor_tensor(eu, bu, mid, ALU.subtract)
                            ins = nc.vector.tensor_tensor(el, mid, bl, ALU.subtract)
                        elif n == len(LEVELS) - 1:
                            m = HCHUNK
                            (el, eu), (bl, bu) = halves(e, m), halves(bc, m)
                            nc.vector.tensor_copy(eu, bu)
                            ins = nc.vector.tensor_tensor(el, bl[:, :, m - 1:m].to_broadcast([P, 16, m]), bl,
                                                          ALU.subtract)
                        else:
                            m = HCHUNK
                            ec = e.rearrange("p h (c l) -> p h c l", c=4)
                            bb = bc.rearrange("p h (c l) -> p h c l", c=4)
                            end = bb[:, :, :, m - 1:m].to_broadcast([P, HGRN_HEADS, 4, m])
                            step(nc.vector.tensor_tensor(ec[:, :, 0:2, :], end[:, :, 0:2, :],
                                                         bb[:, :, 0:2, :], ALU.subtract))
                            nc.vector.tensor_tensor(ec[:, :, 0, :], ec[:, :, 0, :], end[:, :, 1, :], ALU.add)
                            nc.vector.tensor_copy(ec[:, :, 2, :], bb[:, :, 2, :])
                            ins = nc.vector.tensor_tensor(ec[:, :, 3, :], bb[:, :, 3, :], end[:, :, 2, :], ALU.add)
                        ins.then_inc(lev_v, 1)

                    def factors(n):
                        dve.wait_ge(lev_a, n + 1)
                        m = LEVELS[n] if n < len(LEVELS) else P
                        (el, eu), (kl, _), (_, qu) = (halves(v, m) for v in (ebuf[n % 2], kr, qr))
                        nc.vector.tensor_tensor(eu, eu, qu, ALU.mult)
                        nc.vector.tensor_tensor(el, el, kl, ALU.mult).then_inc(lev_q, 1)

                    def merge(n):
                        mask = ident[:, :] if n == 0 else lev[:, n - 1, :]
                        dve.wait_ge(lev_mm, n + 1)
                        if n:
                            dve.wait_ge(att_v, 4 * n)
                        for b in range(4):
                            nc.vector.copy_predicated(
                                att[:, 4 * b:4 * b + 4, :],
                                mask.bitcast(U32).unsqueeze(1).to_broadcast([P, 4, P]),
                                bank[4 * (n % 2) + b][:, :].rearrange("p (m l) -> p m l", m=4)) \
                                .then_inc(att_v, 1)

                    exponents(0)
                    for n in range(len(LEVELS) + 1):
                        if n < len(LEVELS):
                            exponents(n + 1)
                        factors(n)
                        merge(n)
                    for b in range(4):
                        dve.wait_ge(oms, b + 1)
                        nc.vector.tensor_scalar(ovars[:, 2 * b:2 * b + 2, :],
                                                bank[4 + b][:, :].rearrange("p (h t) -> p h t", h=2),
                                                float(D) / P, EPS, ALU.mult, ALU.add).then_inc(ovar, 1)
                    dve.wait_ge(osd, 1)
                    step(nc.vector.reciprocal(ovars, ovars))
                    for b in range(4):
                        ins = nc.vector.scalar_tensor_tensor(
                            out=on_t[:, 2 * b:2 * b + 2, :],
                            in0=bank[b][:, :].rearrange("p (h t) -> p h t", h=2), scalar=par_at("hgrn_g"),
                            in1=ovars[:, 2 * b:2 * b + 2, :], op0=ALU.mult, op1=ALU.mult)
                    step(ins)
                    dve.wait_ge(hg_a, 3)
                    nc.vector.tensor_tensor(on_t, on_t, gr, ALU.mult).then_inc(on, 1)
                    dve.wait_ge(on, 1)
                    acts_lo(on_t, ACTS["hgrn_out"])
                    for m in range(KC):
                        dve.wait_ge(mm_done, FIRST["hgrn_out"] + m + 1)
                        nc.vector.tensor_tensor(x[:, m, :], x[:, m, :], bank[m % BANKS][:, 0:T],
                                                ALU.add).then_inc(evac, 1)
                    dve.wait_ge(evac, EVAC["q1"])

                norm(1 + 2 * layer)
                acts_lo(hn, ACTS[f"q{layer}"])
                tc = [0]

                def own_step(ins, before=[0]):
                    tc[0] += 1
                    ins.then_inc(tk, 1)

                def settle():
                    dve.wait_ge(tk, tk_base + tc[0])
                tk_base = layer * TK_STEPS

                def top16(values, indices, src, spare):
                    n = range(len(src))
                    for i in n:
                        own_step(nc.vector.max(values[i][:, 0:8], src[i]))
                    settle()
                    for i in n:
                        own_step(nc.vector.max_index(indices[i][:, 0:8], values[i][:, 0:8], src[i]))
                        own_step(nc.vector.match_replace(spare[i], values[i][:, 0:8], src[i], -3.0e38))
                    settle()
                    for i in n:
                        own_step(nc.vector.max(values[i][:, 8:16], spare[i]))
                    settle()
                    for i in n:
                        own_step(nc.vector.max_index(indices[i][:, 8:16], values[i][:, 8:16], spare[i]))

                for b in range(NB):
                    dve.wait_ge(sc_a, 8 * layer + 4 * b + 4)
                    if b == 1:
                        dve.wait_ge(lists, 2 * layer + 1)
                    best = lst[:, 2, b * P:(b + 1) * P].rearrange("p (h k) -> p h k", h=PH)
                    posh = pos.rearrange("p (h k) -> p h k", h=PH)
                    for h in range(PH):
                        top16([topv[:, h, c, :] for c in range(2)], [topi[:, h, c, :] for c in range(2)],
                              [sc[:, b, 2 * h + c, :] for c in range(2)], [repl[:, c, :] for c in range(2)])
                        settle()
                        own_step(nc.vector.tensor_tensor(
                            cand.rearrange("p (i j) -> p i j", i=TOPK),
                            topv[:, h, 0, :].unsqueeze(2).to_broadcast([P, TOPK, TOPK]),
                            topv[:, h, 1, :].unsqueeze(1).to_broadcast([P, TOPK, TOPK]), ALU.add))
                        settle()
                        top16([best[:, h, :]], [posh[:, h, :]], [cand], [cand2])
                    settle()
                    own_step(nc.vector.tensor_copy(topf, topi))
                    own_step(nc.vector.tensor_scalar(half[:, 0, :], pos, 4, None, ALU.logical_shift_right))
                    own_step(nc.vector.tensor_scalar(half[:, 1, :], pos, TOPK - 1, None, ALU.bitwise_and))
                    settle()
                    own_step(nc.vector.tensor_copy(halff, half))
                    settle()
                    dve.wait_ge(sc_mm, 8 * layer + 8)
                    for c in range(2):
                        e3 = eq.rearrange("p (n a) -> p n a", a=TOPK)
                        e4 = eq.rearrange("p (h k a) -> p h k a", h=PH, k=TOPK)
                        own_step(nc.vector.tensor_tensor(
                            e3, halff[:, c, :].unsqueeze(2).to_broadcast([P, PH * TOPK, TOPK]),
                            iota[:, 0:TOPK].unsqueeze(1).to_broadcast([P, PH * TOPK, TOPK]), ALU.is_equal))
                        settle()
                        own_step(nc.vector.tensor_tensor(
                            e4, e4, topf[:, :, c, :].unsqueeze(2).to_broadcast([P, PH, TOPK, TOPK]), ALU.mult))
                        settle()
                        own_step(nc.vector.tensor_reduce(lst[:, c, b * P:(b + 1) * P], e3, AX.X, ALU.add))
                        settle()
                    own_step(nc.vector.tensor_copy(small[:, 3, b * PH:(b + 1) * PH], best[:, :, 0]))
                    settle()
                    nc.vector.tensor_tensor(best, best, small[:, 3, b * PH:(b + 1) * PH].unsqueeze(2)
                                            .to_broadcast([P, PH, TOPK]), ALU.subtract).then_inc(lists, 1)
                assert tc[0] == TK_STEPS, tc
                dve.wait_ge(gexp, layer + 1)
                allk = lst[:, 2, :].rearrange("p (n k) -> p n k", k=TOPK)
                step(nc.vector.tensor_reduce(small[:, 4, 0:16], allk, AX.X, ALU.add))
                step(nc.vector.reciprocal(small[:, 4, 0:16], small[:, 4, 0:16]))
                nc.vector.tensor_tensor(allk, allk, small[:, 4, 0:16].unsqueeze(2).to_broadcast([P, 16, TOPK]),
                                        ALU.mult).then_inc(gate_v, 1)
                dve.wait_ge(lt_mm, layer + 1)
                nc.vector.tensor_copy(picks[:, 0:2, :], bank[4][:, :].rearrange("p (a t) -> p a t", a=2))
                nc.vector.tensor_copy(picks[:, 2, :], bank[5][:, 0:T]).then_inc(lt_v, 1)
                dve.wait_ge(lt_v, layer + 1)

                def multiply(grp, b):
                    dve.wait_ge(gate_mm, 64 * layer + grp + 1)
                    v = big[:, :, bass.ds(4 * grp, 4)]
                    nc.vector.tensor_tensor(v, v, bank[b][:, :].rearrange("p (n j) -> p j n", n=4),
                                            ALU.mult).then_inc(gated, 1)

                def gates(i):
                    first = isinstance(i, int) and i == 0
                    for q in range(4):
                        if not (first and q < 2 and layer == 0):
                            dve.wait_ge(gate_mm, 64 * layer + 4 * i + q - 1)
                        for t in range(4):
                            n = 16 * i + 4 * q + t
                            ins = nc.vector.tensor_scalar(oha[:, q % 2, t, :], iota[:, :],
                                                          picks[:, 0, bass.ds(n, 1)],
                                                          picks[:, 2, bass.ds(n, 1)], ALU.is_equal, ALU.mult)
                        ins.then_inc(oha_done, 1)
                        if not (first and q == 0):
                            multiply(4 * i + q - 1, (q + 3) % 4)
                dve.wait_ge(evac, EVAC[f"u{layer}"] + 128)
                gates(0)
                with dve.Fori(1, 16) as i:
                    gates(i)
                multiply(63, 3)

                name = f"v{layer}"
                with dve.Fori(0, COUNT[name] // RAW) as i:
                    for r in range(RAW):
                        dve.wait_ge(hi_done, FIRST[name] + RAW * i + r + 1)
                        nc.vector.tensor_tensor(wlo[:, r, :, :], raw[:, r, :, :], whi[:, r, :, :].bitcast(F32),
                                                ALU.subtract).then_inc(lo_dve, 1)
                add_acc(FIRST[name] + COUNT[name])
            norm(4)


TK_STEPS = NB * (PH * (2 * 5 + 1 + 5) + 4 + 2 * 3 + 1)


def kernel(**inputs):
    import numpy as np
    import concourse.bacc as bacc
    from concourse.bass_utils import run_bass_kernel_spmd as run

    a = {k: np.asarray(v) for k, v in inputs.items()}

    def tiles(w):
        k, n = w.shape
        v = w.reshape(k // D, KC, P, n // P, P).transpose(3, 0, 2, 1, 4)
        return v.reshape(n // P, k // D, P, TILE)

    def column(v):
        return v.reshape(-1, P).T

    def rows(v):
        return np.concatenate([v, np.zeros(P - v.shape[0], v.dtype)])[:, None]

    d_in, n_conv = XT * P, CONV * P
    w_in = a["ssd_w_in"][0]
    w = {
        "ssd_in": tiles(np.concatenate([w_in[:, d_in:d_in + n_conv], w_in[:, :d_in]], axis=1))[:, 0],
        "ssd_out": tiles(a["ssd_w_out"][0]).transpose(1, 0, 2, 3).reshape(16, P, TILE),
        "hgrn_out": tiles(a["hgrn_w_out"][0])[:, 0],
    }
    hw = tiles(a["hgrn_w_in"][0])[:, 0]
    w["hgrn_in"] = np.concatenate([hw[8:16], hw[0:8], hw[16:32]])
    keys = []
    for n in range(2):
        w[f"q{n}"] = tiles(a["peer_w_query"][n])[:, 0]
        u = a["peer_u"][n].reshape(KEYS, KEYS, KC, P)
        w[f"u{n}"] = u.transpose(1, 3, 2, 0).reshape(KEYS, P, TILE)
        w[f"v{n}"] = a["peer_v"][n].reshape(KEYS, KEYS, D).transpose(1, 0, 2)
        keys.append(a["peer_sub_keys"][n].reshape(2 * PH, KEYS, P).transpose(2, 0, 1))
    par = np.concatenate(
        [column(v) for v in (a["mix_norm_g"][0], a["ffn_norm_g"][0], a["mix_norm_g"][1], a["ffn_norm_g"][1],
                             a["final_norm_g"])]
        + [a["ssd_conv_w"][0].reshape(4, CONV, P).transpose(2, 1, 0).reshape(P, 4 * CONV),
           column(a["ssd_conv_b"][0]), column(np.repeat(a["ssd_d_skip"][0], 64)), column(a["ssd_norm_g"][0]),
           column(a["hgrn_lb_logits"][0]), column(a["hgrn_lb_logits"][1]), column(a["hgrn_norm_g"][0]),
           rows(a["ssd_dt_bias"][0]), rows(a["ssd_a_log"][0])], axis=1)
    s, l = np.arange(P)[:, None], np.arange(P)[None, :]
    con = [s == l, np.broadcast_to(l, (P, P)), s <= l]
    con += [(s // (2 * m) == l // (2 * m)) & (s % (2 * m) < m) & (l % (2 * m) >= m) for m in LEVELS]
    arrays = {
        "x_t": a["x"][0].T.reshape(KC, P, T).transpose(1, 0, 2),
        "par": par,
        "con": np.stack(con).astype(np.float32),
        "w_dt": w_in[:, d_in + n_conv:].reshape(KC, P, HEADS).transpose(1, 0, 2),
        **{f"w_{k}": v for k, v in w.items()},
        "keys0": keys[0], "keys1": keys[1],
    }
    arrays = {k: np.ascontiguousarray(v) for k, v in arrays.items()}

    nc = bacc.Bacc("TRN2", target_bir_lowering=False, num_devices=1, dynamic_dma_scratch_size=1024)
    ap = {k: nc.dram_tensor(k, v.shape, F32, kind="ExternalInput").ap() for k, v in arrays.items()}
    out = nc.dram_tensor("out_t", (P, KC, T), F32, kind="ExternalOutput").ap()
    trunk(nc, ap["x_t"], ap["par"], ap["con"], ap["w_dt"], {k: ap[f"w_{k}"] for k in w},
          [ap["keys0"], ap["keys1"]], out)
    r = run(nc, [arrays], core_ids=[0])
    got = r.results[0]["out_t"]
    return np.ascontiguousarray(got.transpose(2, 1, 0).reshape(1, T, D))
```

```python
from contextlib import ExitStack

import concourse.bass as bass
from concourse import mybir

F32 = mybir.dt.float32
F32R = mybir.dt.float32r
U32 = mybir.dt.uint32
ALU = mybir.AluOpType
ACT = mybir.ActivationFunctionType
AX = mybir.AxisListType

P = 128
D = 1024
KC = D // P
T = 256
NB = T // P
TILE = KC * P
EPS = 1e-6

SSD_TILES = 40
CONV = 24
XT = 16
HEADS = 32
GROUPS = 4
HGRN_HEADS = 8
HCHUNK = 64
PH = 8
KEYS = 128
TOPK = 16

RAW = 4
SPL = 4
BANKS = 4

STREAM = [("ssd_in", SSD_TILES), ("ssd_out", 16), ("q0", 16), ("u0", 128), ("v0", 128),
          ("hgrn_in", 32), ("hgrn_out", 8), ("q1", 16), ("u1", 128), ("v1", 128)]
FIRST, POOL_LO, DVE_LO = {}, {}, {}
EVAC = {}
_g = _p = _d = _e = 0
for _n, _c in STREAM:
    FIRST[_n], POOL_LO[_n], DVE_LO[_n], EVAC[_n] = _g, _p, _d, _e
    _g += _c
    if _n[0] == "v":
        _d += _c
    else:
        _p += _c
        _e += 0 if _n == "ssd_out" else _c
COUNT = dict(STREAM)
STAGES = [n for n, _ in STREAM]

PAR = {}
_at = 0
for _n, _c in [("norm_g", 5 * KC), ("conv_w", CONV * 4), ("conv_b", CONV), ("d_skip", XT), ("ssd_g", XT),
               ("lb", 2 * KC), ("hgrn_g", 1), ("dt_bias", 1), ("a_log", 1)]:
    PAR[_n] = (_at, _at + _c)
    _at += _c
NPAR = _at

LEVELS = [1, 2, 4, 8, 16, 32, 64]
CON = {"ident": 0, "iota": 1, "tri": 2, "lev": 3}
NCON = 3 + len(LEVELS)
IN_STREAM = 3

ACTS = {"ssd_in": 1, "y0": 2, "y1": 3, "q0": 4, "hgrn_in": 5, "hgrn_out": 6, "q1": 7}
SCRATCH0 = 72
LISTS_AT = 24


def trunk(nc, x_t, par, con, w_dt, weights, sub_keys, out_t):
    ctx = ExitStack()

    def sb(name, shape, dt=F32):
        return ctx.enter_context(nc.sbuf_tensor(name, shape, dt))

    def sem(name):
        return ctx.enter_context(nc.semaphore(name))

    with ctx:
        big = sb("big", [P, 128, T])
        raw = sb("raw", [P, RAW, KC, P])
        whi = sb("whi", [P, SPL, KC, P], F32R)
        wlo = sb("wlo", [P, SPL, KC, P], F32R)
        x = sb("x", [P, KC, T])
        hhi = sb("hhi", [P, KC, T], F32R)
        hlo = sb("hlo", [P, KC, T], F32R)
        pars = sb("pars", [P, NPAR])
        ident = sb("ident", [P, P])
        iota = sb("iota", [P, P])
        ones = sb("ones", [P, P])
        mean = sb("mean", [P, 2 * HGRN_HEADS - 1])
        zero = sb("zero", [P, 512], mybir.dt.bfloat16)
        picks = sb("picks", [P, 2, T])
        fives = sb("fives", [P, T // 4, 5])
        neg_gate = sb("neg_gate", [P, T // 4])
        oha = sb("oha", [P, 2, 4, P])
        var = sb("var", [P, T])
        rstd = sb("rstd", [P, T])
        wdt = sb("wdt", [P, KC, HEADS])
        small = sb("small", [P, 8, T])
        lbt = sb("lbt", [P, 6, KC])
        aexp = sb("aexp", [HEADS, 1])
        bank = [ctx.enter_context(nc.psum_tensor(f"bank{i}", [P, 512], F32)) for i in range(8)]

        flat = big[:, :, :].rearrange("p a b -> p (a b)")

        def work(at, n, m=1):
            v = flat[:, at:at + n]
            return v if m == 1 else v.rearrange("p (m n) -> p m n", m=m)

        def par_at(name, i=0, rows=P):
            a = PAR[name][0] + i
            return pars[0:rows, a:a + 1]

        def acc(m):
            return bank[4 + m // 2][:, (m % 2) * T:(m % 2 + 1) * T]

        def norm_bank(n):
            return bank[7 if n == 3 else 3][:, 0:T]

        raw_in = [sem(f"raw_in{r}") for r in range(RAW)]
        hi_done = sem("hi_done")
        lo_pool = sem("lo_pool")
        lo_dve = sem("lo_dve")
        mm_done = sem("mm_done")
        evac = sem("evac")
        x_in = sem("x_in")
        par_in = sem("par_in")
        tri_in = sem("tri_in")
        lev_in = sem("lev_in")
        keys_in = sem("keys_in")
        stored = sem("stored")
        ones_set = sem("ones_set")
        sq_done = sem("sq_done")
        ms_done = sem("ms_done")
        var_done = sem("var_done")
        sd_done = sem("sd_done")
        hn_done = sem("hn_done")
        hhi_done = sem("hhi_done")
        hlo_done = sem("hlo_done")
        x_done = sem("x_done")
        own = sem("own")
        pads = sem("pads")
        conv_step = sem("conv_step")
        conv_act = sem("conv_act")
        dt_mm = sem("dt_mm")
        dt_v = sem("dt_v")
        dt_a = sem("dt_a")
        tok_mm = sem("tok_mm")
        tok_v = sem("tok_v")
        xt_mm = sem("xt_mm")
        xt_v = sem("xt_v")
        bt_mm = sem("bt_mm")
        bt_v = sem("bt_v")
        cb_mm = sem("cb_mm")
        cb_v = sem("cb_v")
        seg_mm = sem("seg_mm")
        seg_v = sem("seg_v")
        seg_a = sem("seg_a")
        dec_a = sem("dec_a")
        dec_v = sem("dec_v")
        st_mm = sem("st_mm")
        st_a = sem("st_a")
        z_act = sem("z_act")
        y_mm = sem("y_mm")
        y_v = sem("y_v")
        ysq = sem("ysq")
        yms = sem("yms")
        yvar = sem("yvar")
        ysd = sem("ysd")
        yn = sem("yn")
        hg_a = sem("hg_a")
        hg_v = sem("hg_v")
        hset = sem("hset")
        lb_v = sem("lb_v")
        lb_a = sem("lb_a")
        it_mm = sem("it_mm")
        it_a = sem("it_a")
        lev_v = sem("lev_v")
        lev_a = sem("lev_a")
        lev_q = sem("lev_q")
        lev_mm = sem("lev_mm")
        att_v = sem("att_v")
        att_a = sem("att_a")
        o_mm = sem("o_mm")
        osq = sem("osq")
        oms = sem("oms")
        ovar = sem("ovar")
        osd = sem("osd")
        orec = sem("orec")
        obc = sem("obc")
        on = sem("on")
        sc_mm = sem("sc_mm")
        sc_a = sem("sc_a")
        tk = sem("tk")
        lists = sem("lists")
        gexp = sem("gexp")
        gate_v = sem("gate_v")
        lt_mm = sem("lt_mm")
        lt_v = sem("lt_v")
        oha_done = sem("oha_done")
        dif_done = sem("dif_done")
        dif_sq = sem("dif_sq")
        ohb_done = sem("ohb_done")
        gate_mm = sem("gate_mm")
        gated = sem("gated")
        chi = sem("chi")
        clo = sem("clo")

        sq = work(0, 2048, KC)
        hn = work(2048, 2048, KC)
        zs = work(0, 4096, XT)
        xc = work(4096, 6144, CONV)
        pad = work(10240, CONV * (T + 3), CONV)
        decay = work(10240, 8192).rearrange("p (c h l) -> p c h l", c=NB, h=HEADS)
        ysquare = [work(at, 1024, 4) for at in (22528, 23552, 10240, 11264)]
        yvars = work(30720, 1024, GROUPS)
        xdt = work(18432, 4096).rearrange("p (c m) -> p c m", c=NB)
        xtail = work(22528, 2048)
        cexp = work(24576, 4096, HEADS)
        state = work(28672, 2048, GROUPS)
        btok = work(30720, 512, GROUPS)
        cbm = work(31232, 1024, 2 * GROUPS)
        tok5 = work(32256, 5 * HEADS, 5)
        tri = work(32416, 128)
        b_t, c_t = xc[:, XT:XT + GROUPS, :], xc[:, XT + GROUPS:CONV, :]
        fr = work(0, 2048, KC)
        qr = work(2048, 2048, KC)
        ir = work(4096, 2048, KC)
        gr = work(6144, 2048, KC)
        kr = work(8192, 2048, KC)
        bc = work(10240, 2048, KC)
        ebuf = [work(12288, 2048, KC), work(14336, 2048, KC)]
        att = work(16384, 2048, 2 * HGRN_HEADS)
        att2 = work(18432, 1024, HGRN_HEADS)
        itok = work(19456, 2048, NB)
        on_t = work(21504, 2048, KC)
        oroot = work(30720, T)[0:HGRN_HEADS, :]
        lev = work(23552, 128 * len(LEVELS), len(LEVELS))
        reset = work(24576, 2048, KC)
        sig = work(26624, 2048, KC)
        osquare = work(28672, 2048, KC)
        base = SCRATCH0 * T
        q_t = work(base, 4096, 2 * PH)
        eq = work(base, 2048)
        sk = work(base + 4096, 2048, 2 * PH)
        sc = work(base + 6144, 4096).rearrange("p (b m k) -> p b m k", b=NB, m=2 * PH)
        tkw = base + 10240
        repl = work(tkw, 256, 2)
        cand = work(tkw + 256, 256)
        cand2 = work(tkw + 512, 256)
        topv = work(tkw + 768, 256).rearrange("p (h c k) -> p h c k", h=PH, c=2)
        topi = work(tkw + 1024, 256).bitcast(U32).rearrange("p (h c k) -> p h c k", h=PH, c=2)
        topf = work(tkw + 1280, 256).rearrange("p (h c k) -> p h c k", h=PH, c=2)
        pos = work(tkw + 1536, 128).bitcast(U32)
        half = work(tkw + 1664, 256, 2).bitcast(U32)
        halff = work(tkw + 1920, 256, 2)
        dif = [v[:, :, :].rearrange("p a b -> p (a b)")[:, 5 * P * r:5 * P * (r + 1)]
               .rearrange("p (n k) -> p n k", k=P) for v, r in ((hhi, 0), (hhi, 1), (hhi, 2), (small, 0))]
        ohb = [hlo[:, 2 * r:2 * r + 2, :].rearrange("p a (b k) -> p (a b) k", k=P) for r in range(4)]

        def level_bank(n, b):
            return bank[4 * (n % 2 if n > IN_STREAM else 1) + b]
        lst = small

        def rounds(eng, name, body, first=True, last=False):
            n = COUNT[name] // RAW
            a, b = int(first), n - int(last)
            if first:
                body(0)
            if b > a:
                with eng.Fori(a, b) as i:
                    body(i)
            if last:
                body(n - 1)

        block = ctx.enter_context(nc.Block())

        @block.sync
        def _(sp):
            sp.dma_start(x[:, :, :], x_t).then_inc(x_in, 16)
            sp.dma_start(pars[:, :], par).then_inc(par_in, 16)
            sp.dma_start(ident[:, :], con[CON["ident"]]).then_inc(par_in, 16)
            sp.dma_start(iota[:, :], con[CON["iota"]]).then_inc(par_in, 16)
            sp.dma_start(wdt[:, :, :], w_dt).then_inc(par_in, 16)
            sp.dma_start(tri, con[CON["tri"]]).then_inc(tri_in, 16)

            def load(name, i, r, before):
                if before is not None:
                    lo, count = before
                    sp.wait_ge(lo, count)
                sp.dma_start(raw[:, r, :, :], weights[name][RAW * i + r]
                             .rearrange("p (k c) -> p k c", k=KC)).then_inc(raw_in[r], 16)

            prev = None
            for name in STAGES:
                v = name[0] == "v"
                lo, at = (lo_dve, DVE_LO) if v else (lo_pool, POOL_LO)
                if name in ("q0", "q1"):
                    sp.wait_ge(hlo_done, 2 * ACTS["y1" if name == "q0" else "hgrn_out"])
                    sp.dma_start(sk, sub_keys[int(name[1])]).then_inc(keys_in, 16)

                def body(i):
                    for r in range(RAW):
                        if isinstance(i, int) and i == 0:
                            before = None
                            if prev is not None:
                                plo, pat = (lo_dve, DVE_LO) if prev[0] == "v" else (lo_pool, POOL_LO)
                                before = plo, pat[prev] + COUNT[prev] - RAW + r + 1
                        else:
                            before = lo, at[name] + RAW * i + r - RAW + 1
                        load(name, i, r, before)
                if name == "hgrn_in":
                    body(0)
                    sp.wait_ge(x_done, 8)
                    sp.dma_start(lev, con[CON["lev"]:NCON].rearrange("n p q -> p n q")).then_inc(lev_in, 16)
                    with sp.Fori(1, COUNT[name] // RAW) as i:
                        body(i)
                else:
                    rounds(sp, name, body)
                prev = name
            for e in range(2):
                ks = slice(4 * e, 4 * e + 4)
                sp.wait_ge(hn_done, 9 + e)
                sp.dma_start(out_t[:, ks, :], hn[:, ks, :]).then_inc(stored, 16)
            sp.wait_ge(stored, 32)

        @block.gpsimd
        def _(pool):
            nc.gpsimd.memset(pad[:, :, 0:3], 0.0).then_inc(pads, 1)

            def lo(name, i, r):
                g = FIRST[name] + RAW * i + r
                pool.wait_ge(hi_done, g + 1)
                nc.gpsimd.tensor_tensor(wlo[:, r, :, :], raw[:, r, :, :], whi[:, r, :, :].bitcast(F32),
                                        ALU.subtract).then_inc(lo_pool, 1)

            def los(name, a=0):
                with pool.Fori(a, COUNT[name] // RAW) as i:
                    for r in range(RAW):
                        lo(name, i, r)

            for layer in range(2):
                if layer == 0:
                    los("ssd_in")
                    los("ssd_out")
                else:
                    for r in range(RAW):
                        lo("hgrn_in", 0, r)
                    pool.wait_ge(x_done, 8)
                    nc.gpsimd.memset(reset, 1.0).then_inc(hset, 1)
                    nc.gpsimd.memset(att, 0.0).then_inc(hset, 1)
                    pool.wait_ge(hset, 2)
                    nc.gpsimd.memset(reset.rearrange("p h (c l) -> p (h c) l", l=HCHUNK)[:, :, 0:1],
                                     0.0).then_inc(hset, 1)
                    los("hgrn_in", 1)
                    los("hgrn_out")
                los(f"q{layer}")
                los(f"u{layer}")

                pool.wait_ge(lt_v, layer + 1)
                pool.wait_ge(evac, EVAC[f"u{layer}"] + 128)

                def differences(i):
                    for q in range(4):
                        if not (isinstance(i, int) and i == 0 and layer == 0):
                            pool.wait_ge(ohb_done, 64 * layer + 4 * i + q - 3)
                        n = 4 * i + q
                        nc.gpsimd.tensor_tensor(
                            dif[q], iota[:, :].unsqueeze(1).to_broadcast([P, 5, P]),
                            fives[:, bass.ds(n, 1), :].rearrange("p a b -> p (a b)").unsqueeze(2)
                            .to_broadcast([P, 5, P]), ALU.subtract).then_inc(dif_done, 1)
                differences(0)
                with pool.Fori(1, 16) as i:
                    differences(i)

                name = f"v{layer}"

                def c_lo(i):
                    for r in range(RAW):
                        j = RAW * i + r
                        pool.wait_ge(chi, 128 * layer + j + 1)
                        nc.gpsimd.tensor_tensor(hlo[:, r, :], big[:, bass.ds(j, 1), :].rearrange("p a b -> p (a b)"),
                                                hhi[:, r, :].bitcast(F32), ALU.subtract).then_inc(clo, 1)
                with pool.Fori(0, 32) as i:
                    c_lo(i)

        @block.scalar
        def _(act):
            def hi(g, r):
                act.wait_ge(raw_in[r], 16 * (g // RAW + 1) if isinstance(g, int) else 4 * (g - r) + 16)
                if not isinstance(g, int) or g >= SPL:
                    act.wait_ge(mm_done, g - SPL + 1)
                nc.scalar.activation(whi[:, r, :, :], raw[:, r, :, :], ACT.Copy).then_inc(hi_done, 1)

            def stream(name, out, a=0, b=None, last=False):
                def body(i, end=False):
                    for r in range(RAW):
                        g = FIRST[name] + RAW * i + r
                        if not end or r < 2:
                            hi(g + 2, (r + 2) % RAW)
                        out(RAW * i + r, r, g)
                b = COUNT[name] // RAW if b is None else b
                if a == 0 and name == "ssd_in" or b - a == 1:
                    body(a)
                    a += 1
                if b - int(last) > a:
                    with act.Fori(a, b - int(last)) as i:
                        body(i)
                if last:
                    body(b - 1, end=True)

            def copy_to(dst):
                def out(t, r, g):
                    act.wait_ge(mm_done, g + 1)
                    nc.scalar.activation(dst(t), bank[r][:, 0:T], ACT.Copy).then_inc(evac, 1)
                return out

            def col(t):
                return big[:, bass.ds(t, 1), :].rearrange("p a b -> p (a b)")

            def norm(n, ready, values):
                for b in range(4):
                    act.wait_ge(ready, values[b])
                    nc.scalar.activation(sq[:, 2 * b:2 * b + 2, :], x[:, 2 * b:2 * b + 2, :],
                                         ACT.Square).then_inc(sq_done, 1)
                act.wait_ge(var_done, n + 1)
                nc.scalar.activation(rstd[:, :], var[:, :], ACT.Sqrt).then_inc(sd_done, 1)

            def acts_hi(src, ready, *values):
                for e in range(2):
                    act.wait_ge(ready, values[e])
                    nc.scalar.activation(hhi[:, 4 * e:4 * e + 4, :], src[:, 4 * e:4 * e + 4, :],
                                         ACT.Copy).then_inc(hhi_done, 1)

            nc.scalar.preload_act_table(ACT.Sqrt)
            hi(0, 0)
            hi(1, 1)
            norm(0, x_in, [16] * 4)
            acts_hi(hn, hn_done, 1, 2)
            def to_pad(t):
                return pad[:, bass.ds(t, 1), 3:T + 3].rearrange("p a b -> p (a b)")

            def conv_silu(i):
                act.wait_ge(conv_step, 16 * i + 16)
                v = xc[:, bass.ds(4 * i, 4), :]
                nc.scalar.activation(v, v, ACT.Silu).then_inc(conv_act, 1)

            stream("ssd_in", copy_to(to_pad), 0, 1)
            nc.scalar.preload_act_table_set("natural_log_exp_and_others")
            act.wait_ge(par_in, 64)
            act.wait_ge(dt_v, 1)
            nc.scalar.activation(small[0:HEADS, 1, :], small[0:HEADS, 1, :], ACT.Exp).then_inc(dt_a, 1)
            nc.scalar.activation(aexp[:, :], par_at("a_log", 0, HEADS), ACT.Exp).then_inc(dt_a, 1)
            act.wait_ge(lb_v, 1)
            nc.scalar.activation(lbt[:, 0:2, :], lbt[:, 0:2, :], ACT.Exp).then_inc(lb_a, 1)
            stream("ssd_in", copy_to(to_pad), 1, 2)
            act.wait_ge(dt_v, 2)
            nc.scalar.activation(small[0:HEADS, 3, :], small[0:HEADS, 2, :], ACT.Ln).then_inc(dt_a, 1)
            stream("ssd_in", copy_to(to_pad), 2, 3)
            act.wait_ge(dt_v, 3)
            nc.scalar.activation(small[0:HEADS, 3, 0:P], small[0:HEADS, 3, 0:P], ACT.Exp).then_inc(dt_a, 1)
            nc.scalar.preload_act_table(ACT.Silu)
            stream("ssd_in", copy_to(to_pad), 3, CONV // RAW)
            for q in range(CONV // 4 - 2):
                conv_silu(q)
            stream("ssd_in", copy_to(lambda t: col(t - CONV)), CONV // RAW)
            for q in range(CONV // 4 - 2, CONV // 4):
                conv_silu(q)
            act.wait_ge(evac, SSD_TILES)
            nc.scalar.activation(zs, zs, ACT.Silu).then_inc(z_act, 1)
            for q in range(HEADS // 2):
                act.wait_ge(seg_v, q + 1)
                src = bank[q % 4][:, :].rearrange("p (h t) -> p h t", h=2)[:, :, P:T]
                nc.scalar.activation(cexp[:, 2 * q:2 * q + 2, :], src, ACT.Exp).then_inc(seg_a, 1)
                if q % 4 == 3:
                    g = q // 4
                    for c in range(NB):
                        v = decay[:, c, 8 * g:8 * g + 8, :]
                        nc.scalar.activation(v, v, ACT.Exp).then_inc(dec_a, 1)
            act.wait_ge(st_mm, 1)
            for g in range(GROUPS):
                nc.scalar.activation(state[:, g, :], bank[4 + g][:, :], ACT.Copy).then_inc(st_a, 1)
            nc.scalar.preload_act_table(ACT.Sqrt)

            def y_square(g):
                act.wait_ge(y_v, g + 1)
                nc.scalar.activation(ysquare[g], xc[:, 4 * g:4 * g + 4, :], ACT.Square).then_inc(ysq, 1)

            def y_root(e):
                act.wait_ge(yvar, e + 1)
                v = yvars[:, 2 * e:2 * e + 2, :]
                nc.scalar.activation(v, v, ACT.Sqrt).then_inc(ysd, 1)

            def out_hi(i, rs=range(RAW)):
                for r in rs:
                    hi(FIRST["ssd_out"] + RAW * i + r + 2, (r + 2) % RAW)
            for g in range(3):
                y_square(g)
            y_root(0)
            acts_hi(xc[:, 0:KC, :], yn, 1, 2)
            y_square(3)
            out_hi(0, range(2))
            y_root(1)
            out_hi(0, range(2, RAW))
            out_hi(1)
            act.wait_ge(mm_done, FIRST["ssd_out"] + KC)
            acts_hi(xc[:, KC:XT, :], yn, 3, 4)
            with act.Fori(2, 4) as i:
                out_hi(i)

            for layer in range(2):
                if layer == 1:
                    nc.scalar.preload_act_table(ACT.Sqrt)
                    norm(2, x_done, range(5, 9))
                    acts_hi(hn, hn_done, 5, 6)

                    def level(n):
                        act.wait_ge(lev_v, n + 1)
                        nc.scalar.activation(ebuf[n % 2], ebuf[n % 2], ACT.Exp).then_inc(lev_a, 1)
                    nc.scalar.preload_act_table(ACT.Sigmoid)
                    stream("hgrn_in", copy_to(col), 0, 3)
                    act.wait_ge(evac, EVAC["hgrn_in"] + KC)
                    nc.scalar.activation(sig, fr, ACT.Sigmoid).then_inc(hg_a, 1)
                    nc.scalar.activation(kr, fr, ACT.Sigmoid, scale=-1.0).then_inc(hg_a, 1)
                    stream("hgrn_in", copy_to(col), 3, 4)
                    nc.scalar.preload_act_table_set("natural_log_exp_and_others")
                    act.wait_ge(hg_v, 1)
                    nc.scalar.activation(fr, sig, ACT.Ln).then_inc(hg_a, 1)
                    for n in range(IN_STREAM):
                        stream("hgrn_in", copy_to(col), 4 + n, 5 + n)
                        level(n)
                    stream("hgrn_in", copy_to(col), 4 + IN_STREAM)
                    for b in range(NB * 2):
                        act.wait_ge(it_mm, b + 1)
                        nc.scalar.activation(itok[:, b // 2, 512 * (b % 2):512 * (b % 2) + 512],
                                             bank[b][:, :], ACT.Copy).then_inc(it_a, 1)
                    for n in range(IN_STREAM, len(LEVELS) + 1):
                        level(n)
                    act.wait_ge(evac, EVAC["hgrn_out"])
                    nc.scalar.activation(gr, gr, ACT.Silu).then_inc(hg_a, 1)
                    nc.scalar.preload_act_table(ACT.Sqrt)
                    act.wait_ge(lev_mm, len(LEVELS) + 2)
                    n = len(LEVELS) + 1
                    for b in range(2):
                        nc.scalar.activation(att2[:, 4 * b:4 * b + 4, :],
                                             level_bank(n, b)[:, :].rearrange("p (h l) -> p h l", h=4),
                                             ACT.Copy).then_inc(att_a, 1)
                    for b in range(4):
                        act.wait_ge(o_mm, b + 1)
                        nc.scalar.activation(osquare[:, 2 * b:2 * b + 2, :],
                                             bank[b][:, :].rearrange("p (h l) -> p h l", h=2),
                                             ACT.Square).then_inc(osq, 1)
                    act.wait_ge(ovar, 1)
                    nc.scalar.activation(oroot, oroot, ACT.Sqrt).then_inc(osd, 1)
                    acts_hi(on_t, on, 2, 4)
                    with act.Fori(0, 2) as i:
                        for r in range(RAW):
                            hi(FIRST["hgrn_out"] + RAW * i + r + 2, (r + 2) % RAW)

                nc.scalar.preload_act_table(ACT.Sqrt)
                if layer == 0:
                    norm(1, x_done, range(1, 5))
                else:
                    norm(3, evac, [EVAC["q1"] - KC + 2 * b + 2 for b in range(4)])
                acts_hi(hn, hn_done, 4 * layer + 3, 4 * layer + 4)
                stream(f"q{layer}", copy_to(lambda t: col(t + SCRATCH0)))
                for n in range(2 * 4):
                    act.wait_ge(sc_mm, 8 * layer + n + 1)
                    b, m = divmod(n, 4)
                    nc.scalar.activation(sc[:, b, 4 * m:4 * m + 4, :],
                                         bank[4 + n % 4][:, :].rearrange("p (m k) -> p m k", m=4),
                                         ACT.Copy).then_inc(sc_a, 1)
                nc.scalar.preload_act_table(ACT.Gelu)

                def gelu(t, r, g):
                    act.wait_ge(mm_done, g + 1)
                    nc.scalar.activation(col(t), bank[r][:, 0:T], ACT.Gelu).then_inc(evac, 1)
                stream(f"u{layer}", gelu, 0, SCRATCH0 // RAW)
                act.wait_ge(lists, 2 * layer + 2)
                nc.scalar.activation(lst[:, 2, :], lst[:, 2, :], ACT.Exp).then_inc(gexp, 1)
                nc.scalar.preload_act_table(ACT.Gelu)
                stream(f"u{layer}", gelu, SCRATCH0 // RAW)

                def square(n, q):
                    act.wait_ge(dif_done, n + 1)
                    v = dif[q]
                    nc.scalar.activation(v, v.bitcast(F32), ACT.Square).then_inc(dif_sq, 1)

                def one_hots(i, last=False):
                    first = isinstance(i, int) and i == 0 and layer == 0
                    for q in range(4):
                        n = 64 * layer + 4 * i + q
                        if not (last and q == 3):
                            square(n + 1, (q + 1) % 4)
                        v = dif[q]
                        if not first:
                            act.wait_ge(gate_mm, n - 3)
                        act.wait_ge(dif_sq, n + 1)
                        nc.scalar.activation(ohb[q], v[:, 0:4, :].bitcast(F32), ACT.Relu, bias=1.0, scale=-1.0)
                        if not (first and q < 2):
                            act.wait_ge(gate_mm, n - 1)
                        nc.scalar.activation(oha[:, q % 2, 3, :], v[:, 4, :].bitcast(F32), ACT.Relu,
                                             bias=picks[:, 1, bass.ds(16 * i + 4 * q + 3, 1)],
                                             scale=neg_gate[:, bass.ds(4 * i + q, 1)]).then_inc(ohb_done, 1)
                square(64 * layer, 0)
                one_hots(0)
                with act.Fori(1, 15) as i:
                    one_hots(i)
                one_hots(15, last=True)

                def c_hi(j, r):
                    nc.scalar.activation(hhi[:, r, :], col(j), ACT.Copy).then_inc(chi, 1)
                act.wait_ge(gated, 64 * layer + 64)
                name = f"v{layer}"
                c_hi(0, 0)
                c_hi(1, 1)

                def v_round(i, end=False):
                    for r in range(RAW):
                        g = FIRST[name] + RAW * i + r
                        last = layer == 1
                        if not (end and r >= 2 and last):
                            hi(g + 2, (r + 2) % RAW)
                        if not (end and r >= 2):
                            act.wait_ge(mm_done, g + 2 - RAW + 1)
                            c_hi(RAW * i + r + 2, (r + 2) % RAW)
                with act.Fori(0, COUNT[name] // RAW - 1) as i:
                    v_round(i)
                v_round(COUNT[name] // RAW - 1, end=True)
            nc.scalar.preload_act_table(ACT.Sqrt)
            norm(4, x_done, range(9, 13))

        @block.tensor
        def _(pe):
            def split(out, r, start, stop, acts=None, **kw):
                n = 0
                for k in range(KC):
                    if acts and k % 4 == 0:
                        pe.wait_ge(hhi_done, 2 * ACTS[acts] - 1 + k // 4)
                        pe.wait_ge(hlo_done, 2 * ACTS[acts] - 1 + k // 4)
                    for w, h in ((whi, hhi), (whi, hlo), (wlo, hhi)):
                        ins = nc.tensor.matmul(out, w[:, r, k, :], h[:, k, :], start=start and n == 0,
                                               stop=stop and n == 3 * KC - 1, **kw)
                        n += 1
                return ins

            def tile_ready(name, i, r):
                g = FIRST[name] + RAW * i + r
                pe.wait_ge(hi_done, g + 1)
                if name[0] == "v":
                    pe.wait_ge(lo_dve, DVE_LO[name] + RAW * i + r + 1)
                else:
                    pe.wait_ge(lo_pool, POOL_LO[name] + RAW * i + r + 1)

            def project(name, a=0, b=None):
                def body(i):
                    for r in range(RAW):
                        tile_ready(name, i, r)
                        e = EVAC[name] + RAW * i + r
                        if not isinstance(e, int) or e >= BANKS:
                            pe.wait_ge(evac, e - BANKS + 1)
                        first = name in ACTS and isinstance(i, int) and i + r == 0
                        split(bank[r][:, 0:T], r, True, True, name if first else None).then_inc(mm_done, 1)
                b = COUNT[name] // RAW if b is None else b
                if name in ACTS and a == 0 or b - a == 1:
                    body(a)
                    a += 1
                if b > a:
                    with pe.Fori(a, b) as i:
                        body(i)

            def clear():
                for b in range(4, 8):
                    nc.tensor.matmul(bank[b][:, :], zero[:, 0:P], zero[:, :], start=True, stop=True,
                                     skip_group_check=True)

            def norm(n):
                for k in range(KC):
                    if k % 2 == 0:
                        pe.wait_ge(sq_done, 4 * n + k // 2 + 1)
                    ins = nc.tensor.matmul(norm_bank(n), ones[:, :], sq[:, k, :], start=k == 0,
                                           stop=k == KC - 1)
                ins.then_inc(ms_done, 1)

            pe.wait_ge(ones_set, 2)
            norm(0)
            project("ssd_in", 0, 1)
            pe.wait_ge(hn_done, 2)
            pe.wait_ge(par_in, 64)
            for k in range(KC):
                ins = nc.tensor.matmul(bank[4][0:HEADS, 0:T], wdt[:, k, :], hn[:, k, :], start=k == 0,
                                       stop=k == KC - 1)
            ins.then_inc(dt_mm, 1)
            project("ssd_in", 1)
            pe.wait_ge(dt_v, 4)
            idn = ident[0:HEADS, 0:HEADS]
            for n, (slot, c) in enumerate([(6, 0), (6, 1), (7, 0), (7, 1), (3, 0)]):
                ins = nc.tensor.transpose(bank[4][:, T + HEADS * n:T + HEADS * (n + 1)],
                                          small[0:HEADS, slot, c * P:(c + 1) * P], idn)
            ins.then_inc(tok_mm, 1)
            pe.wait_ge(conv_act, CONV // 4)
            pe.wait_ge(evac, SSD_TILES)
            for n in range(8):
                c, q = divmod(n, 4)
                b = (0, 1, 2, 3, 5, 6, 7, 0)[n]
                if n == 7:
                    pe.wait_ge(xt_v, 1)
                for m in range(4):
                    ins = nc.tensor.transpose(bank[b][:, P * m:P * (m + 1)],
                                              xc[:, 4 * q + m, c * P:(c + 1) * P], ident[:, :])
                ins.then_inc(xt_mm, 1)
            pe.wait_ge(tok_v, 1)
            for g in range(GROUPS):
                ins = nc.tensor.transpose(bank[4][:, P * g:P * (g + 1)], b_t[:, g, 0:P], ident[:, :])
            ins.then_inc(bt_mm, 1)
            for c in range(NB):
                pe.wait_ge(xt_v, 5 + c)
                for g in range(GROUPS):
                    t = slice(c * P, (c + 1) * P)
                    ins = nc.tensor.matmul(bank[5 + c][:, P * g:P * (g + 1)], b_t[:, g, t], c_t[:, g, t],
                                           start=True, stop=True)
                ins.then_inc(cb_mm, 1)
            pe.wait_ge(xt_v, 8)
            for q in range(HEADS // 2):
                if q >= 4:
                    pe.wait_ge(seg_v, q - 3)
                    pe.wait_ge(seg_a, q - 3)
                for e in range(2):
                    h = 2 * q + e
                    ins = nc.tensor.matmul(bank[q % 4][:, e * T:(e + 1) * T],
                                           ident[0:HEADS, h:h + 1].to_broadcast([HEADS, P]),
                                           small[0:HEADS, 7, :], start=True, stop=True)
                ins.then_inc(seg_mm, 1)
            pe.wait_ge(bt_v, 1)
            pe.wait_ge(cb_v, 2)
            for g in range(GROUPS):
                ins = nc.tensor.matmul(bank[4 + g][:, :], btok[:, g, :], xtail[:, 512 * g:512 * (g + 1)],
                                       start=True, stop=True)
            ins.then_inc(st_mm, 1)
            pe.wait_ge(seg_v, 16)
            pe.wait_ge(seg_a, 16)
            pe.wait_ge(st_a, GROUPS)
            def y_tiles(a, b):
                for n in range(a, b):
                    if n % 2 == 0:
                        pe.wait_ge(dec_v, 3 * (n // 2) + 3)
                    for e in range(2):
                        m = 2 * n + e
                        for hh in range(2):
                            h = 2 * m + hh
                            rows = slice(64 * hh, 64 * hh + 64)
                            for c in range(NB):
                                out = bank[n][rows, e * T + c * P:e * T + (c + 1) * P]
                                ins = nc.tensor.matmul(out, xdt[:, c, 64 * h:64 * h + 64], decay[:, c, h, :],
                                                       start=True, stop=c == 0)
                                if c == 1:
                                    hg = 64 * (h % 8)
                                    ins = nc.tensor.matmul(out, state[:, h // 8, hg:hg + 64], cexp[:, h, :],
                                                           start=False, stop=True)
                    ins.then_inc(y_mm, 1)

            def y_means(e):
                for g in range(2 * e, 2 * e + 2):
                    pe.wait_ge(ysq, g + 1)
                    for m in range(4):
                        ins = nc.tensor.matmul(bank[e][:, (g % 2) * T:(g % 2 + 1) * T], ones[:, :],
                                               ysquare[g][:, m, :], start=m == 0, stop=m == 3)
                ins.then_inc(yms, 1)

            def accumulate(i, rs=range(RAW)):
                for r in rs:
                    m = RAW * (i % 2) + r
                    tile_ready("ssd_out", i, r)
                    split(acc(m), r, False, True, f"y{i // 2}" if m == 0 else None,
                          skip_group_check=True).then_inc(mm_done, 1)
            y_tiles(0, 6)
            y_means(0)
            y_tiles(6, 8)
            pe.wait_ge(y_v, 4)
            clear()
            accumulate(0, range(1))
            y_means(1)
            accumulate(0, range(1, RAW))
            accumulate(1)
            accumulate(2)
            accumulate(3)

            for layer in range(2):
                if layer == 1:
                    norm(2)

                    def level(n):
                        if n == 0:
                            pe.wait_ge(hg_v, 3)
                            kk, qq = kr, qr
                        else:
                            pe.wait_ge(lev_q, n)
                            kk = qq = ebuf[(n - 1) % 2]
                        if 1 <= n <= IN_STREAM:
                            pe.wait_ge(att_v, 4 * n)
                        elif n > IN_STREAM + 1:
                            pe.wait_ge(att_v, 4 * (n - 1))
                        for b in range(4):
                            if n == len(LEVELS) + 1 and b >= 2:
                                break
                            for m in range(4):
                                if n <= len(LEVELS):
                                    h, blk = divmod(4 * b + m, 2)
                                    ks = qs = slice(blk * P, (blk + 1) * P)
                                else:
                                    h, ks, qs = 4 * b + m, slice(0, P), slice(P, T)
                                ins = nc.tensor.matmul(level_bank(n, b)[:, P * m:P * (m + 1)],
                                                       kk[:, h, ks], qq[:, h, qs], start=True, stop=True)
                        ins.then_inc(lev_mm, 1)

                    project("hgrn_in", 0, 5)
                    for n in range(IN_STREAM):
                        level(n)
                        project("hgrn_in", 5 + n, 6 + n)
                    pe.wait_ge(evac, EVAC["hgrn_out"])
                    for n in range(4):
                        b, part = divmod(n, 2)
                        for m in range(4):
                            ins = nc.tensor.transpose(bank[n][:, P * m:P * (m + 1)],
                                                      ir[:, 4 * part + m, b * P:(b + 1) * P], ident[:, :])
                        ins.then_inc(it_mm, 1)
                    for n in range(IN_STREAM, len(LEVELS) + 2):
                        if n == IN_STREAM + 1:
                            pe.wait_ge(it_a, 4)
                        level(n)
                    pe.wait_ge(att_v, 4 * (len(LEVELS) + 1))
                    pe.wait_ge(att_a, 2)
                    for b in range(4):
                        for e in range(2):
                            h = 2 * b + e
                            v = slice(P * h, P * h + P)
                            o0 = bank[b][:, e * T:e * T + P]
                            o1 = bank[b][:, e * T + P:(e + 1) * T]
                            nc.tensor.matmul(o0, itok[:, 0, v], att[:, 2 * h, :], start=True, stop=True)
                            nc.tensor.matmul(o1, itok[:, 1, v], att[:, 2 * h + 1, :], start=True, stop=False)
                            ins = nc.tensor.matmul(o1, itok[:, 0, v], att2[:, h, :], start=False, stop=True)
                        ins.then_inc(o_mm, 1)
                    for h in range(HGRN_HEADS):
                        if h % 2 == 0:
                            pe.wait_ge(osq, h // 2 + 1)
                        at = HGRN_HEADS - 1 - h
                        ins = nc.tensor.matmul(bank[4][0:HGRN_HEADS, 0:T], mean[:, at:at + HGRN_HEADS],
                                               osquare[:, h, :], start=h == 0, stop=h == HGRN_HEADS - 1)
                    ins.then_inc(oms, 1)
                    pe.wait_ge(orec, 1)
                    for h in range(HGRN_HEADS):
                        ins = nc.tensor.matmul(bank[4 + h // 2][:, (h % 2) * T:(h % 2 + 1) * T],
                                               ident[0:HGRN_HEADS, h:h + 1].to_broadcast([HGRN_HEADS, P]),
                                               oroot, start=True, stop=True)
                        if h % 2:
                            ins.then_inc(obc, 1)
                    project("hgrn_out")

                norm(1 + 2 * layer)
                project(f"q{layer}")
                pe.wait_ge(keys_in, 16 * layer + 16)
                pe.wait_ge(evac, EVAC[f"u{layer}"])
                for n in range(8):
                    if n >= 4:
                        pe.wait_ge(sc_a, 8 * layer + n - 3)
                    b, q = divmod(n, 4)
                    for m in range(4):
                        ins = nc.tensor.matmul(bank[4 + n % 4][:, P * m:P * (m + 1)],
                                               q_t[:, 4 * q + m, b * P:(b + 1) * P], sk[:, 4 * q + m, :],
                                               start=True, stop=True)
                    ins.then_inc(sc_mm, 1)
                project(f"u{layer}", 0, LISTS_AT)
                pe.wait_ge(sc_a, 8 * layer + 8)
                for n in range(6):
                    kind, b = divmod(n, 2)
                    if n == 4:
                        pe.wait_ge(gate_v, layer + 1)
                    ins = nc.tensor.transpose(bank[4 + n // 4][:, P * (n % 4):P * (n % 4 + 1)],
                                              lst[:, kind, b * P:(b + 1) * P], ident[:, :])
                ins.then_inc(lt_mm, 1)
                project(f"u{layer}", LISTS_AT)

                pe.wait_ge(evac, EVAC[f"u{layer}"] + 128)

                def gates(i):
                    for q in range(4):
                        n = 64 * layer + 4 * i + q
                        pe.wait_ge(oha_done, n + 1)
                        pe.wait_ge(ohb_done, n + 1)
                        if not (isinstance(i, int) and i == 0 and layer == 0):
                            pe.wait_ge(gated, n - 3)
                        for t in range(4):
                            ins = nc.tensor.matmul(bank[q][:, P * t:P * (t + 1)], oha[:, q % 2, t, :],
                                                   ohb[q][:, t, :].bitcast(F32), start=True, stop=True)
                        ins.then_inc(gate_mm, 1)
                gates(0)
                with pe.Fori(1, 16) as i:
                    gates(i)

                pe.wait_ge(lt_v, layer + 1)
                clear()
                name = f"v{layer}"

                def contract(i):
                    for r in range(RAW):
                        tile_ready(name, i, r)
                        pe.wait_ge(chi, 128 * layer + RAW * i + r + 1)
                        pe.wait_ge(clo, 128 * layer + RAW * i + r + 1)
                        for m in range(KC):
                            for w, h in ((whi, hhi), (whi, hlo), (wlo, hhi)):
                                ins = nc.tensor.matmul(acc(m), w[:, r, m, :], h[:, r, :], start=False,
                                                       stop=True, skip_group_check=True)
                        ins.then_inc(mm_done, 1)
                with pe.Fori(0, 32) as i:
                    contract(i)
            norm(4)

        @block.vector
        def _(dve):
            count = [0]

            def step(ins):
                count[0] += 1
                ins.then_inc(own, 1)
                dve.wait_ge(own, count[0])

            def norm(n, split=True):
                dve.wait_ge(ms_done, n + 1)
                nc.vector.tensor_scalar(var[:, :], norm_bank(n), EPS, None, ALU.add).then_inc(var_done, 1)
                dve.wait_ge(sd_done, n + 1)
                step(nc.vector.reciprocal(rstd[:, :], rstd[:, :]))
                for k in range(KC):
                    ins = nc.vector.scalar_tensor_tensor(out=hn[:, k, :], in0=x[:, k, :],
                                                         scalar=par_at("norm_g", n * KC + k),
                                                         in1=rstd[:, :], op0=ALU.mult, op1=ALU.mult)
                    if k % 4 == 3:
                        ins.then_inc(hn_done, 1)

            def acts_lo(src, value):
                for e in range(2):
                    ks = slice(4 * e, 4 * e + 4)
                    dve.wait_ge(hhi_done, 2 * value - 1 + e)
                    nc.vector.tensor_tensor(hlo[:, ks, :], src[:, ks, :], hhi[:, ks, :].bitcast(F32),
                                            ALU.subtract).then_inc(hlo_done, 1)

            def add_acc(value):
                dve.wait_ge(mm_done, value)
                for b in range(4):
                    v = x[:, 2 * b:2 * b + 2, :]
                    nc.vector.tensor_tensor(v, v, bank[4 + b][:, :].rearrange("p (m t) -> p m t", m=2),
                                            ALU.add).then_inc(x_done, 1)

            nc.vector.memset(ones[:, :], 1.0 / D).then_inc(ones_set, 1)
            nc.vector.memset(zero[:, :], 0.0).then_inc(ones_set, 1)
            step(nc.vector.memset(mean[:, :], 0.0))
            at = HGRN_HEADS - 1
            nc.vector.memset(mean[:, at:at + 1], 1.0 / P).then_inc(ones_set, 1)
            dve.wait_ge(par_in, 64)
            a = PAR["lb"][0]
            lg = pars[:, a:a + 2 * KC].rearrange("p (l k) -> p l k", l=2)
            step(nc.vector.tensor_tensor(lbt[:, 2, :], lg[:, 0, :], lg[:, 1, :], ALU.max))
            nc.vector.tensor_tensor(lbt[:, 0:2, :], lg, lbt[:, 2:3, :].to_broadcast([P, 2, KC]),
                                    ALU.subtract).then_inc(lb_v, 1)

            norm(0)
            acts_lo(hn, ACTS["ssd_in"])
            dve.wait_ge(dt_mm, 1)
            sm = lambda i: small[0:HEADS, i, :]
            v, u, w, t3, d, z, dt, acs = (sm(i) for i in range(8))
            step(nc.vector.tensor_scalar(v, bank[4][0:HEADS, 0:T], par_at("dt_bias", 0, HEADS), None, ALU.add))
            step(nc.vector.tensor_scalar(u, v, -1.0, None, ALU.mult))
            nc.vector.tensor_tensor(u, u, v, ALU.min).then_inc(dt_v, 1)
            dve.wait_ge(dt_a, 2)
            nc.vector.tensor_scalar(w, u, 1.0, None, ALU.add).then_inc(dt_v, 1)
            dve.wait_ge(dt_v, 2)
            step(nc.vector.tensor_scalar(d, w, -1.0, None, ALU.add))
            step(nc.vector.tensor_scalar(z, d, 0.0, None, ALU.is_equal))
            step(nc.vector.tensor_tensor(d, d, z, ALU.add))
            step(nc.vector.reciprocal(d, d))
            step(nc.vector.tensor_tensor(z, z, u, ALU.mult))
            dve.wait_ge(dt_a, 3)
            step(nc.vector.tensor_tensor(t3, t3, u, ALU.mult))
            step(nc.vector.tensor_tensor(t3, t3, d, ALU.mult))
            step(nc.vector.tensor_tensor(t3, t3, z, ALU.add))
            step(nc.vector.scalar_tensor_tensor(out=dt, in0=v, scalar=0.0, in1=t3, op0=ALU.max, op1=ALU.add))
            step(nc.vector.tensor_scalar(d, dt, aexp[:, :], -1.0, ALU.mult, ALU.mult))
            step(nc.vector.memset(z, 1.0))
            step(nc.vector.memset(z.rearrange("p (c l) -> p c l", l=P)[:, :, 0:1], 0.0))
            step(nc.vector.tensor_tensor_scan(acs, z, d, 0.0, ALU.mult, ALU.add))
            nc.vector.tensor_scalar(t3[:, 0:P], acs[:, 0:P], -1.0, acs[:, P - 1:P], ALU.mult,
                                    ALU.add).then_inc(dt_v, 1)
            dve.wait_ge(dt_a, 4)
            nc.vector.tensor_tensor(t3[:, 0:P], t3[:, 0:P], dt[:, 0:P], ALU.mult).then_inc(dt_v, 1)
            dve.wait_ge(lb_a, 1)
            step(nc.vector.tensor_tensor(lbt[:, 2, :], lbt[:, 0, :], lbt[:, 1, :], ALU.add))
            step(nc.vector.reciprocal(lbt[:, 2, :], lbt[:, 2, :]))
            step(nc.vector.tensor_tensor(lbt[:, 0:2, :], lbt[:, 0:2, :],
                                         lbt[:, 2:3, :].to_broadcast([P, 2, KC]), ALU.mult))
            step(nc.vector.tensor_tensor(lbt[:, 3, :], lbt[:, 0, :], lbt[:, 1, :], ALU.add))
            step(nc.vector.tensor_tensor(lbt[:, 3, :], lbt[:, 3, :], lbt[:, 0, :], ALU.subtract))
            step(nc.vector.tensor_scalar(lbt[:, 4, :], lbt[:, 3, :], -1.0, 1.0, ALU.mult, ALU.add))
            dve.wait_ge(pads, 1)
            for i in range(CONV // 4):
                dve.wait_ge(evac, 4 * i + 4)
                for tap in range(4):
                    if tap:
                        dve.wait_ge(conv_step, 16 * i + 4 * tap)
                    for m in range(4 * i, 4 * i + 4):
                        src = pad[:, m, 3 - tap:3 - tap + T]
                        cw = par_at("conv_w", 4 * m + 3 - tap)
                        if tap == 0:
                            ins = nc.vector.tensor_scalar(xc[:, m, :], src, cw, par_at("conv_b", m),
                                                          ALU.mult, ALU.add)
                        else:
                            ins = nc.vector.scalar_tensor_tensor(out=xc[:, m, :], in0=src, scalar=cw,
                                                                 in1=xc[:, m, :], op0=ALU.mult, op1=ALU.add)
                        ins.then_inc(conv_step, 1)
            dve.wait_ge(tok_mm, 1)
            nc.vector.tensor_copy(tok5, bank[4][:, T:T + 5 * HEADS].rearrange("p (n h) -> p n h", n=5)) \
                .then_inc(tok_v, 1)
            dve.wait_ge(tok_v, 1)
            for n in range(8):
                c, q = divmod(n, 4)
                b = (0, 1, 2, 3, 5, 6, 7, 0)[n]
                dve.wait_ge(xt_mm, n + 1)
                src = bank[b][:, :].rearrange("p (h v) -> p h v", h=8)
                outs = [(xdt[:, c, 512 * q:512 * (q + 1)], c)] + [(xtail[:, 512 * q:512 * (q + 1)], 4)] * (c == 0)
                for out, slot in outs:
                    by = tok5[:, slot, 8 * q:8 * q + 8].unsqueeze(2).to_broadcast([P, 8, 64])
                    ins = nc.vector.tensor_tensor(out.rearrange("p (h v) -> p h v", h=8), src, by, ALU.mult)
                ins.then_inc(xt_v, 1)
            dve.wait_ge(bt_mm, 1)
            nc.vector.tensor_copy(btok, bank[4][:, :].rearrange("p (g n) -> p g n", g=GROUPS)).then_inc(bt_v, 1)
            dve.wait_ge(tri_in, 16)
            for c in range(NB):
                dve.wait_ge(cb_mm, c + 1)
                nc.vector.tensor_tensor(cbm[:, 4 * c:4 * c + 4, :],
                                        bank[5 + c][:, :].rearrange("p (g l) -> p g l", g=GROUPS),
                                        tri.unsqueeze(1).to_broadcast([P, GROUPS, P]), ALU.mult) \
                    .then_inc(cb_v, 1)
            for q in range(HEADS // 2):
                dve.wait_ge(seg_mm, q + 1)
                for e in range(2):
                    h = 2 * q + e
                    for c in range(NB):
                        ins = nc.vector.tensor_scalar(decay[:, c, h, :],
                                                      bank[q % 4][:, e * T + c * P:e * T + (c + 1) * P],
                                                      tok5[:, 2 + c, h:h + 1], 0.0, ALU.subtract, ALU.min)
                ins.then_inc(seg_v, 1)
            dve.wait_ge(cb_v, 2)
            for g in range(GROUPS):
                hs = slice(8 * g, 8 * g + 8)
                dve.wait_ge(dec_a, 2 * g + 2)
                for c in range(NB):
                    v = decay[:, c, hs, :]
                    nc.vector.tensor_tensor(v, v, cbm[:, 4 * c + g, :].unsqueeze(1).to_broadcast([P, 8, P]),
                                            ALU.mult).then_inc(dec_v, 1)
                v = cexp[:, hs, :]
                nc.vector.tensor_tensor(v, v, c_t[:, g, P:T].unsqueeze(1).to_broadcast([P, 8, P]),
                                        ALU.mult).then_inc(dec_v, 1)
            def y_tiles(a, b):
                for n in range(a, b):
                    dve.wait_ge(y_mm, n + 1)
                    for e in range(2):
                        m = 2 * n + e
                        ins = nc.vector.scalar_tensor_tensor(out=xc[:, m, :], in0=xc[:, m, :],
                                                             scalar=par_at("d_skip", m),
                                                             in1=bank[n][:, e * T:(e + 1) * T],
                                                             op0=ALU.mult, op1=ALU.add)
                    if n % 2:
                        step(ins)
                        if n == 1:
                            dve.wait_ge(z_act, 1)
                        v = xc[:, 2 * n - 2:2 * n + 2, :]
                        nc.vector.tensor_tensor(v, v, zs[:, 2 * n - 2:2 * n + 2, :], ALU.mult).then_inc(y_v, 1)

            def y_vars(e):
                dve.wait_ge(yms, e + 1)
                nc.vector.tensor_scalar(yvars[:, 2 * e:2 * e + 2, :], bank[e][:, :].rearrange("p (g t) -> p g t", g=2),
                                        float(D) / 512, EPS, ALU.mult, ALU.add).then_inc(yvar, 1)

            def y_norm(e):
                dve.wait_ge(ysd, e + 1)
                v = yvars[:, 2 * e:2 * e + 2, :]
                step(nc.vector.reciprocal(v, v))
                for m in range(KC * e, KC * e + KC):
                    ins = nc.vector.scalar_tensor_tensor(out=xc[:, m, :], in0=xc[:, m, :],
                                                         scalar=par_at("ssd_g", m), in1=yvars[:, m // 4, :],
                                                         op0=ALU.mult, op1=ALU.mult)
                    if m % 4 == 3:
                        ins.then_inc(yn, 1)
            y_tiles(0, 6)
            y_vars(0)
            y_norm(0)
            y_tiles(6, 8)
            acts_lo(xc[:, 0:KC, :], ACTS["y0"])
            y_vars(1)
            y_norm(1)
            acts_lo(xc[:, KC:XT, :], ACTS["y1"])
            add_acc(FIRST["q0"])

            for layer in range(2):
                if layer == 1:
                    norm(2)
                    acts_lo(hn, ACTS["hgrn_in"])
                    dve.wait_ge(hg_a, 2)
                    for h in range(HGRN_HEADS):
                        ins = nc.vector.tensor_scalar(sig[:, h, :], sig[:, h, :], lbt[:, 4, h:h + 1],
                                                      lbt[:, 3, h:h + 1], ALU.mult, ALU.add)
                    ins.then_inc(hg_v, 1)
                    for h in range(HGRN_HEADS):
                        ins = nc.vector.tensor_scalar(kr[:, h, :], kr[:, h, :], lbt[:, 4, h:h + 1], None,
                                                      ALU.mult)
                    ins.then_inc(hg_v, 1)
                    dve.wait_ge(hg_a, 3)
                    dve.wait_ge(hset, 3)
                    nc.vector.tensor_tensor_scan(bc.rearrange("p h l -> p (h l)"),
                                                 reset.rearrange("p h l -> p (h l)"),
                                                 fr.rearrange("p h l -> p (h l)"), 0.0,
                                                 ALU.mult, ALU.add).then_inc(hg_v, 1)
                    dve.wait_ge(hg_v, 3)
                    dve.wait_ge(lev_in, 16)

                    def halves(v, m):
                        w = v.rearrange("p h l -> p (h l)").rearrange("p (n l) -> p n l", l=2 * m)
                        return w[:, :, 0:m], w[:, :, m:2 * m]

                    def exponents(n):
                        if n >= 2:
                            dve.wait_ge(lev_mm, n)
                        e = ebuf[n % 2]
                        if n < len(LEVELS) - 1:
                            m = LEVELS[n]
                            (el, eu), (bl, bu) = halves(e, m), halves(bc, m)
                            mid = bl[:, :, m - 1:m].to_broadcast([P, 2048 // (2 * m), m])
                            nc.vector.tensor_tensor(eu, bu, mid, ALU.subtract)
                            ins = nc.vector.tensor_tensor(el, mid, bl, ALU.subtract)
                        elif n == len(LEVELS) - 1:
                            m = HCHUNK
                            (el, eu), (bl, bu) = halves(e, m), halves(bc, m)
                            nc.vector.tensor_copy(eu, bu)
                            ins = nc.vector.tensor_tensor(el, bl[:, :, m - 1:m].to_broadcast([P, 16, m]), bl,
                                                          ALU.subtract)
                        else:
                            m = HCHUNK
                            ec = e.rearrange("p h (c l) -> p h c l", c=4)
                            bb = bc.rearrange("p h (c l) -> p h c l", c=4)
                            end = bb[:, :, :, m - 1:m].to_broadcast([P, HGRN_HEADS, 4, m])
                            step(nc.vector.tensor_tensor(ec[:, :, 0:2, :], end[:, :, 0:2, :],
                                                         bb[:, :, 0:2, :], ALU.subtract))
                            nc.vector.tensor_tensor(ec[:, :, 0, :], ec[:, :, 0, :], end[:, :, 1, :], ALU.add)
                            nc.vector.tensor_copy(ec[:, :, 2, :], bb[:, :, 2, :])
                            ins = nc.vector.tensor_tensor(ec[:, :, 3, :], bb[:, :, 3, :], end[:, :, 2, :], ALU.add)
                        ins.then_inc(lev_v, 1)

                    def factors(n):
                        dve.wait_ge(lev_a, n + 1)
                        m = LEVELS[n] if n < len(LEVELS) else P
                        (el, eu), (kl, _), (_, qu) = (halves(v, m) for v in (ebuf[n % 2], kr, qr))
                        nc.vector.tensor_tensor(eu, eu, qu, ALU.mult)
                        nc.vector.tensor_tensor(el, el, kl, ALU.mult).then_inc(lev_q, 1)

                    def merge(n):
                        mask = ident[:, :] if n == 0 else lev[:, n - 1, :]
                        dve.wait_ge(lev_mm, n + 1)
                        if n:
                            dve.wait_ge(att_v, 4 * n)
                        for b in range(4):
                            nc.vector.copy_predicated(
                                att[:, 4 * b:4 * b + 4, :],
                                mask.bitcast(U32).unsqueeze(1).to_broadcast([P, 4, P]),
                                level_bank(n, b)[:, :].rearrange("p (m l) -> p m l", m=4)) \
                                .then_inc(att_v, 1)

                    exponents(0)
                    for n in range(len(LEVELS) + 1):
                        factors(n)
                        if n < len(LEVELS):
                            exponents(n + 1)
                        merge(n)
                    dve.wait_ge(hg_a, 4)
                    for b in range(4):
                        dve.wait_ge(osq, b + 1)
                        ins = nc.vector.scalar_tensor_tensor(
                            out=on_t[:, 2 * b:2 * b + 2, :],
                            in0=bank[b][:, :].rearrange("p (h t) -> p h t", h=2), scalar=par_at("hgrn_g"),
                            in1=gr[:, 2 * b:2 * b + 2, :], op0=ALU.mult, op1=ALU.mult)
                    step(ins)
                    dve.wait_ge(oms, 1)
                    nc.vector.tensor_scalar(oroot, bank[4][0:HGRN_HEADS, 0:T], EPS, None, ALU.add).then_inc(ovar, 1)
                    dve.wait_ge(osd, 1)
                    nc.vector.reciprocal(oroot, oroot).then_inc(orec, 1)
                    for b in range(4):
                        dve.wait_ge(obc, b + 1)
                        v = on_t[:, 2 * b:2 * b + 2, :]
                        nc.vector.tensor_tensor(v, v, bank[4 + b][:, :].rearrange("p (h t) -> p h t", h=2),
                                                ALU.mult).then_inc(on, 1)
                    acts_lo(on_t, ACTS["hgrn_out"])
                    for m in range(KC):
                        dve.wait_ge(mm_done, FIRST["hgrn_out"] + m + 1)
                        nc.vector.tensor_tensor(x[:, m, :], x[:, m, :], bank[m % BANKS][:, 0:T],
                                                ALU.add).then_inc(evac, 1)
                    dve.wait_ge(evac, EVAC["q1"])

                norm(1 + 2 * layer)
                acts_lo(hn, ACTS[f"q{layer}"])
                tc = [0]

                def own_step(ins, before=[0]):
                    tc[0] += 1
                    ins.then_inc(tk, 1)

                def settle():
                    dve.wait_ge(tk, tk_base + tc[0])
                tk_base = layer * TK_STEPS

                def top16(values, indices, src, spare):
                    n = range(len(src))
                    for i in n:
                        own_step(nc.vector.max(values[i][:, 0:8], src[i]))
                    settle()
                    for i in n:
                        own_step(nc.vector.max_index(indices[i][:, 0:8], values[i][:, 0:8], src[i]))
                        own_step(nc.vector.match_replace(spare[i], values[i][:, 0:8], src[i], -3.0e38))
                    settle()
                    for i in n:
                        own_step(nc.vector.max(values[i][:, 8:16], spare[i]))
                    settle()
                    for i in n:
                        own_step(nc.vector.max_index(indices[i][:, 8:16], values[i][:, 8:16], spare[i]))

                for b in range(NB):
                    dve.wait_ge(sc_a, 8 * layer + 4 * b + 4)
                    if b == 1:
                        dve.wait_ge(lists, 2 * layer + 1)
                    best = lst[:, 2, b * P:(b + 1) * P].rearrange("p (h k) -> p h k", h=PH)
                    posh = pos.rearrange("p (h k) -> p h k", h=PH)
                    for h in range(PH):
                        top16([topv[:, h, c, :] for c in range(2)], [topi[:, h, c, :] for c in range(2)],
                              [sc[:, b, 2 * h + c, :] for c in range(2)], [repl[:, c, :] for c in range(2)])
                        settle()
                        own_step(nc.vector.tensor_tensor(
                            cand.rearrange("p (i j) -> p i j", i=TOPK),
                            topv[:, h, 0, :].unsqueeze(2).to_broadcast([P, TOPK, TOPK]),
                            topv[:, h, 1, :].unsqueeze(1).to_broadcast([P, TOPK, TOPK]), ALU.add))
                        settle()
                        top16([best[:, h, :]], [posh[:, h, :]], [cand], [cand2])
                    settle()
                    own_step(nc.vector.tensor_copy(topf, topi))
                    own_step(nc.vector.tensor_scalar(half[:, 0, :], pos, 4, None, ALU.logical_shift_right))
                    own_step(nc.vector.tensor_scalar(half[:, 1, :], pos, TOPK - 1, None, ALU.bitwise_and))
                    settle()
                    own_step(nc.vector.tensor_copy(halff, half))
                    settle()
                    dve.wait_ge(sc_mm, 8 * layer + 8)
                    for c in range(2):
                        e3 = eq.rearrange("p (n a) -> p n a", a=TOPK)
                        e4 = eq.rearrange("p (h k a) -> p h k a", h=PH, k=TOPK)
                        own_step(nc.vector.tensor_tensor(
                            e3, halff[:, c, :].unsqueeze(2).to_broadcast([P, PH * TOPK, TOPK]),
                            iota[:, 0:TOPK].unsqueeze(1).to_broadcast([P, PH * TOPK, TOPK]), ALU.is_equal))
                        settle()
                        own_step(nc.vector.tensor_tensor(
                            e4, e4, topf[:, :, c, :].unsqueeze(2).to_broadcast([P, PH, TOPK, TOPK]), ALU.mult))
                        settle()
                        own_step(nc.vector.tensor_reduce(lst[:, c, b * P:(b + 1) * P], e3, AX.X, ALU.add))
                        settle()
                    own_step(nc.vector.tensor_copy(small[:, 3, b * PH:(b + 1) * PH], best[:, :, 0]))
                    settle()
                    nc.vector.tensor_tensor(best, best, small[:, 3, b * PH:(b + 1) * PH].unsqueeze(2)
                                            .to_broadcast([P, PH, TOPK]), ALU.subtract).then_inc(lists, 1)
                assert tc[0] == TK_STEPS, tc
                dve.wait_ge(gexp, layer + 1)
                allk = lst[:, 2, :].rearrange("p (n k) -> p n k", k=TOPK)
                step(nc.vector.tensor_reduce(small[:, 4, 0:16], allk, AX.X, ALU.add))
                step(nc.vector.reciprocal(small[:, 4, 0:16], small[:, 4, 0:16]))
                nc.vector.tensor_tensor(allk, allk, small[:, 4, 0:16].unsqueeze(2).to_broadcast([P, 16, TOPK]),
                                        ALU.mult).then_inc(gate_v, 1)
                dve.wait_ge(lt_mm, layer + 1)
                nc.vector.tensor_copy(fives[:, :, 0:4], bank[4][:, T:2 * T].rearrange("p (n t) -> p n t", t=4))
                nc.vector.tensor_copy(fives[:, :, 4], bank[4][:, 0:T].rearrange("p (n t) -> p n t", t=4)[:, :, 3])
                nc.vector.tensor_scalar(neg_gate[:, :], bank[5][:, 0:T].rearrange("p (n t) -> p n t", t=4)[:, :, 3],
                                        -1.0, None, ALU.mult)
                nc.vector.tensor_copy(picks[:, 0, :], bank[4][:, 0:T])
                nc.vector.tensor_copy(picks[:, 1, :], bank[5][:, 0:T]).then_inc(lt_v, 1)
                dve.wait_ge(lt_v, layer + 1)

                def multiply(grp, b):
                    dve.wait_ge(gate_mm, 64 * layer + grp + 1)
                    v = big[:, :, bass.ds(4 * grp, 4)]
                    nc.vector.tensor_tensor(v, v, bank[b][:, :].rearrange("p (n j) -> p j n", n=4),
                                            ALU.mult).then_inc(gated, 1)

                def gates(i):
                    first = isinstance(i, int) and i == 0
                    for q in range(4):
                        if not (first and q < 2 and layer == 0):
                            dve.wait_ge(gate_mm, 64 * layer + 4 * i + q - 1)
                        for t in range(3):
                            n = 16 * i + 4 * q + t
                            ins = nc.vector.tensor_scalar(oha[:, q % 2, t, :], iota[:, :],
                                                          picks[:, 0, bass.ds(n, 1)],
                                                          picks[:, 1, bass.ds(n, 1)], ALU.is_equal, ALU.mult)
                        ins.then_inc(oha_done, 1)
                        if not (first and q == 0):
                            multiply(4 * i + q - 1, (q + 3) % 4)
                dve.wait_ge(evac, EVAC[f"u{layer}"] + 128)
                gates(0)
                with dve.Fori(1, 16) as i:
                    gates(i)
                multiply(63, 3)

                name = f"v{layer}"
                with dve.Fori(0, COUNT[name] // RAW) as i:
                    for r in range(RAW):
                        dve.wait_ge(hi_done, FIRST[name] + RAW * i + r + 1)
                        nc.vector.tensor_tensor(wlo[:, r, :, :], raw[:, r, :, :], whi[:, r, :, :].bitcast(F32),
                                                ALU.subtract).then_inc(lo_dve, 1)
                add_acc(FIRST[name] + COUNT[name])
            norm(4)


TK_STEPS = NB * (PH * (2 * 5 + 1 + 5) + 4 + 2 * 3 + 1)


def kernel(**inputs):
    import numpy as np
    import concourse.bacc as bacc
    from concourse.bass_utils import run_bass_kernel_spmd as run

    a = {k: np.asarray(v) for k, v in inputs.items()}

    def tiles(w):
        k, n = w.shape
        v = w.reshape(k // D, KC, P, n // P, P).transpose(3, 0, 2, 1, 4)
        return v.reshape(n // P, k // D, P, TILE)

    def column(v):
        return v.reshape(-1, P).T

    def rows(v):
        return np.concatenate([v, np.zeros(P - v.shape[0], v.dtype)])[:, None]

    d_in, n_conv = XT * P, CONV * P
    w_in = a["ssd_w_in"][0]
    w = {
        "ssd_in": tiles(np.concatenate([w_in[:, d_in:d_in + n_conv], w_in[:, :d_in]], axis=1))[:, 0],
        "ssd_out": tiles(a["ssd_w_out"][0]).transpose(1, 0, 2, 3).reshape(16, P, TILE),
        "hgrn_out": tiles(a["hgrn_w_out"][0])[:, 0],
    }
    hw = tiles(a["hgrn_w_in"][0])[:, 0]
    w["hgrn_in"] = np.concatenate([hw[8:16], hw[0:8], hw[16:32]])
    keys = []
    for n in range(2):
        w[f"q{n}"] = tiles(a["peer_w_query"][n])[:, 0]
        u = a["peer_u"][n].reshape(KEYS, KEYS, KC, P)
        w[f"u{n}"] = u.transpose(1, 3, 2, 0).reshape(KEYS, P, TILE)
        w[f"v{n}"] = a["peer_v"][n].reshape(KEYS, KEYS, D).transpose(1, 0, 2)
        keys.append(a["peer_sub_keys"][n].reshape(2 * PH, KEYS, P).transpose(2, 0, 1))
    par = np.concatenate(
        [column(v) for v in (a["mix_norm_g"][0], a["ffn_norm_g"][0], a["mix_norm_g"][1], a["ffn_norm_g"][1],
                             a["final_norm_g"])]
        + [a["ssd_conv_w"][0].reshape(4, CONV, P).transpose(2, 1, 0).reshape(P, 4 * CONV),
           column(a["ssd_conv_b"][0]), column(np.repeat(a["ssd_d_skip"][0], 64)), column(a["ssd_norm_g"][0]),
           column(a["hgrn_lb_logits"][0]), column(a["hgrn_lb_logits"][1]), column(a["hgrn_norm_g"][0]),
           rows(a["ssd_dt_bias"][0]), rows(a["ssd_a_log"][0])], axis=1)
    s, l = np.arange(P)[:, None], np.arange(P)[None, :]
    con = [s == l, np.broadcast_to(l, (P, P)), s <= l]
    con += [(s // (2 * m) == l // (2 * m)) & (s % (2 * m) < m) & (l % (2 * m) >= m) for m in LEVELS]
    arrays = {
        "x_t": a["x"][0].T.reshape(KC, P, T).transpose(1, 0, 2),
        "par": par,
        "con": np.stack(con).astype(np.float32),
        "w_dt": w_in[:, d_in + n_conv:].reshape(KC, P, HEADS).transpose(1, 0, 2),
        **{f"w_{k}": v for k, v in w.items()},
        "keys0": keys[0], "keys1": keys[1],
    }
    arrays = {k: np.ascontiguousarray(v) for k, v in arrays.items()}

    nc = bacc.Bacc("TRN2", target_bir_lowering=False, num_devices=1, dynamic_dma_scratch_size=1024)
    ap = {k: nc.dram_tensor(k, v.shape, F32, kind="ExternalInput").ap() for k, v in arrays.items()}
    out = nc.dram_tensor("out_t", (P, KC, T), F32, kind="ExternalOutput").ap()
    trunk(nc, ap["x_t"], ap["par"], ap["con"], ap["w_dt"], {k: ap[f"w_{k}"] for k in w},
          [ap["keys0"], ap["keys1"]], out)
    r = run(nc, [arrays], core_ids=[0])
    got = r.results[0]["out_t"]
    return np.ascontiguousarray(got.transpose(2, 1, 0).reshape(1, T, D))
```
